# Optimizing a Trainium2 kernel written in Bass

```python
import math
import jax, jax.numpy as jnp
from jax import lax
import numpy as np

D_MODEL = 2048
BATCH = 1
SEQ = 256
DEPTH = 1

HEAD_DIM = 128
DIL_PATTERNS = ((128, 1), (512, 4), (2048, 16))
N_DIL_GROUPS = 3
HEADS_PER_DIL_GROUP = 4
N_HEADS_A = N_DIL_GROUPS * HEADS_PER_DIL_GROUP
WIDTH_A = N_HEADS_A * HEAD_DIM
WIDTH_A_OUT = HEADS_PER_DIL_GROUP * HEAD_DIM
BAND_BLOCK = 128
N_HEADS_B = 8
WIDTH_B = N_HEADS_B * HEAD_DIM
N_IDX_HEADS = 16
IDX_DIM = 64
TOPK_MAX = 256
QUERY_BLOCK = 128
N_HEADS_TOTAL = N_HEADS_A + N_HEADS_B
REL_BUCKETS = 32
REL_MAX_DIST = 2048
D_FF = -(-8 * D_MODEL // (3 * 256)) * 256
RMS_EPS = 1e-6
PROJ_WIDTHS = (WIDTH_A, WIDTH_A, WIDTH_A, WIDTH_B, WIDTH_B, WIDTH_B,
               N_IDX_HEADS * IDX_DIM, IDX_DIM, N_IDX_HEADS, D_MODEL, D_MODEL)
D_IN = 3 * WIDTH_A + 3 * WIDTH_B + N_IDX_HEADS * IDX_DIM + IDX_DIM + N_IDX_HEADS + 2 * D_MODEL

kernel_name = "gated_dilated_dsa_hybrid"

def rms_norm(x, g):
    xf = x.astype(jnp.float32)
    y = xf * lax.rsqrt(jnp.mean(xf * xf, axis=-1, keepdims=True) + RMS_EPS)
    return (y * g.astype(jnp.float32)).astype(x.dtype)

def t5_bucket(dist):
    n = jnp.maximum(dist, 0)
    max_exact = REL_BUCKETS // 2
    nf = jnp.maximum(n, 1).astype(jnp.float32)
    large = max_exact + (jnp.log(nf / max_exact) / math.log(REL_MAX_DIST / max_exact)
                         * (REL_BUCKETS - max_exact)).astype(jnp.int32)
    large = jnp.minimum(large, REL_BUCKETS - 1)
    return jnp.where(n < max_exact, n, large)

def proj_split_points():
    pts, acc = [], 0
    for w in PROJ_WIDTHS[:-1]:
        acc += w
        pts.append(acc)
    return pts

def dilated_window_attention(q, k, v, dilation, steps, bias_table):
    B, S, H, Dh = q.shape
    span = dilation * BAND_BLOCK
    n_blk = -(-S // span)
    s_pad = n_blk * span

    def to_strided(a):
        a = jnp.pad(a, ((0, 0), (0, s_pad - S), (0, 0), (0, 0)))
        a = a.reshape(B, n_blk, BAND_BLOCK, dilation, H, Dh)
        return a.transpose(0, 3, 4, 1, 2, 5)

    def with_prev(a):
        prev = jnp.pad(a, ((0, 0), (0, 0), (0, 0), (1, 0), (0, 0), (0, 0)))[:, :, :, :-1]
        return jnp.concatenate([prev, a], axis=4)

    qs = to_strided(q)
    kb = with_prev(to_strided(k))
    vb = with_prev(to_strided(v))

    qi = jnp.arange(BAND_BLOCK)[:, None]
    kj = jnp.arange(2 * BAND_BLOCK)[None, :]
    delta = qi + BAND_BLOCK - kj
    band = (delta >= 0) & (delta <= steps)
    has_prev = (jnp.arange(n_blk) > 0)[:, None, None]
    mask = band[None] & (has_prev | (kj >= BAND_BLOCK)[None])
    bias = bias_table[t5_bucket(delta * dilation)].astype(jnp.float32).transpose(2, 0, 1)

    s = jnp.einsum('brhnqe,brhnke->brhnqk', qs, kb,
                   preferred_element_type=jnp.float32) * (Dh ** -0.5)
    s = s + bias[None, None, :, None]
    s = jnp.where(mask[None, None, None], s, -jnp.inf)
    m = jnp.max(s, axis=-1, keepdims=True)
    p = jnp.exp(s - m)
    l = jnp.sum(p, axis=-1)
    o = jnp.einsum('brhnqk,brhnke->brhnqe', p.astype(v.dtype), vb,
                   preferred_element_type=jnp.float32) / l[..., None]
    lse = m[..., 0] + jnp.log(l)
    o = o.transpose(0, 3, 4, 1, 2, 5).reshape(B, s_pad, H, Dh)[:, :S]
    lse = lse.transpose(0, 3, 4, 1, 2).reshape(B, s_pad, H)[:, :S]
    return o, lse

def dsa_attention(q, k, v, q_idx, k_idx, w_idx, bias_table):
    B, S, H, Dh = q.shape
    topk = min(TOPK_MAX, S // 4)
    nb = S // QUERY_BLOCK
    key_pos = jnp.arange(S)

    def blocks(a):
        return jnp.moveaxis(a.reshape((B, nb, QUERY_BLOCK) + a.shape[2:]), 1, 0)

    def one_block(args):
        qb, qib, wib, t0 = args
        tq = t0 + jnp.arange(QUERY_BLOCK)
        dots = jnp.einsum('bqhe,bse->bqhs', qib, k_idx,
                          preferred_element_type=jnp.float32) * (IDX_DIM ** -0.5)
        score = jnp.einsum('bqhs,bqh->bqs', jax.nn.relu(dots),
                           wib.astype(jnp.float32) * (N_IDX_HEADS ** -0.5))
        score = jnp.where(key_pos[None, None, :] <= tq[None, :, None], score, -jnp.inf)
        _, sel = lax.top_k(score, topk)
        valid = sel <= tq[None, :, None]
        kg = jax.vmap(lambda a, i: a[i])(k, sel)
        vg = jax.vmap(lambda a, i: a[i])(v, sel)
        bias = bias_table[t5_bucket(tq[None, :, None] - sel)].astype(jnp.float32)
        s = jnp.einsum('bqhe,bqkhe->bhqk', qb, kg,
                       preferred_element_type=jnp.float32) * (Dh ** -0.5)
        s = s + bias.transpose(0, 3, 1, 2)
        s = jnp.where(valid[:, None], s, -jnp.inf)
        p = jax.nn.softmax(s, axis=-1)
        return jnp.einsum('bhqk,bqkhe->bqhe', p.astype(v.dtype), vg,
                          preferred_element_type=jnp.float32)

    t0s = jnp.arange(nb, dtype=jnp.int32) * QUERY_BLOCK
    out = lax.map(one_block, (blocks(q), blocks(q_idx), blocks(w_idx), t0s))
    return jnp.moveaxis(out, 0, 1).reshape(B, S, H * Dh)

def setup_inputs(seed: int = 0) -> dict:
    key = jax.random.key(seed)
    ks = jax.random.split(key, 13)
    f32 = jnp.float32

    def nrm(k, shape, fan_in):
        return jax.random.normal(k, shape, f32) * (fan_in ** -0.5)

    return {
        "x": jax.random.normal(ks[0], (BATCH, SEQ, D_MODEL), f32),
        "w_in": nrm(ks[1], (DEPTH, D_MODEL, D_IN), D_MODEL),
        "w_out_a": nrm(ks[2], (DEPTH, WIDTH_A_OUT, D_MODEL), WIDTH_A_OUT),
        "w_out_b": nrm(ks[3], (DEPTH, WIDTH_B, D_MODEL), WIDTH_B),
        "w_out": nrm(ks[4], (DEPTH, D_MODEL, D_MODEL), D_MODEL),
        "w_ff_gate": nrm(ks[5], (DEPTH, D_MODEL, D_FF), D_MODEL),
        "w_ff_up": nrm(ks[6], (DEPTH, D_MODEL, D_FF), D_MODEL),
        "w_ff_down": nrm(ks[7], (DEPTH, D_FF, D_MODEL), D_FF),
        "g_mix": 1.0 + 0.02 * jax.random.normal(ks[8], (DEPTH, D_MODEL), f32),
        "g_ffn": 1.0 + 0.02 * jax.random.normal(ks[9], (DEPTH, D_MODEL), f32),
        "g_final": 1.0 + 0.02 * jax.random.normal(ks[10], (D_MODEL,), f32),
        "rel_bias": 0.2 * jax.random.normal(ks[11], (REL_BUCKETS, N_HEADS_TOTAL), f32),
    }

def reference(x, w_in, w_out_a, w_out_b, w_out, w_ff_gate, w_ff_up, w_ff_down,
              g_mix, g_ffn, g_final, rel_bias):
    B, S, _ = x.shape
    splits = proj_split_points()
    for layer in range(DEPTH):
        h = rms_norm(x, g_mix[layer])
        proj = h @ w_in[layer]
        qa, ka, va, qb, kb, vb, qi, ki, wi, gate_a, gate_b = jnp.split(proj, splits, axis=-1)

        grp = (B, S, N_DIL_GROUPS, HEADS_PER_DIL_GROUP, HEAD_DIM)
        qa, ka, va = qa.reshape(grp), ka.reshape(grp), va.reshape(grp)
        outs, lses = [], []
        for g, (window, dilation) in enumerate(DIL_PATTERNS):
            cols = rel_bias[:, g * HEADS_PER_DIL_GROUP:(g + 1) * HEADS_PER_DIL_GROUP]
            o, lse = dilated_window_attention(qa[:, :, g], ka[:, :, g], va[:, :, g],
                                              dilation, window // dilation, cols)
            outs.append(o)
            lses.append(lse)
        wts = jax.nn.softmax(jnp.stack(lses), axis=0)
        y_a = jnp.sum(wts[..., None] * jnp.stack(outs), axis=0)
        y_a = y_a.reshape(B, S, WIDTH_A_OUT).astype(x.dtype)

        hb = (B, S, N_HEADS_B, HEAD_DIM)
        y_b = dsa_attention(qb.reshape(hb), kb.reshape(hb), vb.reshape(hb),
                            qi.reshape(B, S, N_IDX_HEADS, IDX_DIM), ki, wi,
                            rel_bias[:, N_HEADS_A:]).astype(x.dtype)

        merged = (jax.nn.sigmoid(gate_a) * (y_a @ w_out_a[layer])
                  + jax.nn.sigmoid(gate_b) * (y_b @ w_out_b[layer]))
        x = x + merged @ w_out[layer]

        h = rms_norm(x, g_ffn[layer])
        x = x + (jax.nn.silu(h @ w_ff_gate[layer]) * (h @ w_ff_up[layer])) @ w_ff_down[layer]
    return rms_norm(x, g_final)


_drawn_inputs = setup_inputs


def setup_inputs(seed=0):
    import zlib

    import numpy as np

    out = dict(_drawn_inputs(seed))
    spreads = {}
    factors = {'g_mix': 3.304, 'g_ffn': 3.824, 'g_final': 2.866}
    for name, (base, spread) in spreads.items():
        noise = np.random.default_rng([zlib.crc32(name.encode()), seed]).standard_normal(out[name].shape)
        drawn = base * np.exp(spread * noise) if base else spread * noise
        out[name] = __import__('jax').numpy.asarray(drawn.astype(out[name].dtype))
    for name, factor in factors.items():
        out[name] = (out[name] * factor).astype(out[name].dtype)
    return out
```

```python
import concourse.bass as bass
from concourse import mybir
from contextlib import ExitStack
import numpy as np

P = 128
SEQ = 256
BLK = SEQ // P
D = 2048
KT = D // P
HD = 128
N_GROUP_A, QUAD = 3, 4
N_QUAD_B = 2
N_QUAD = N_GROUP_A + N_QUAD_B
QW = QUAD * HD
WIDTH_A = N_GROUP_A * QW
WIDTH_B = N_QUAD_B * QW
N_IDX, IDX = 16, 64
D_FF = 5632
BUCKETS = 32
N_HEADS = N_QUAD * QUAD
TOPK = 64
EPS = 1e-6
NEG = -1e30
TAKEN = -3e38
COL_Q_A, COL_K_A, COL_V_A = 0, WIDTH_A, 2 * WIDTH_A
COL_Q_B = 3 * WIDTH_A
COL_K_B, COL_V_B = COL_Q_B + WIDTH_B, COL_Q_B + 2 * WIDTH_B
COL_QI = COL_Q_B + 3 * WIDTH_B
COL_KI = COL_QI + N_IDX * IDX
KIW = IDX + N_IDX
COL_GA = COL_KI + KIW
COL_GB = COL_GA + D
NC_ = 512
N_OUT = D // NC_
N_SLAB = D_FF // NC_
SKEW = 3 * P
RING = 4
AHEAD = RING - 1

IDX_AT, IDX_LEN = 0, 24
QUAD_AT, QUAD_LEN = 24, 24
MERGE0_AT, MERGE0_LEN = QUAD_AT + N_QUAD * QUAD_LEN, 24
MERGE_AT, MERGE_LEN = MERGE0_AT + MERGE0_LEN, 32
WOUT_AT, WOUT_LEN = MERGE_AT + (N_OUT - 1) * MERGE_LEN, 8
FFN0_AT, FFN0_LEN = WOUT_AT + WOUT_LEN, 16
FFN_AT, FFN_LEN = FFN0_AT + FFN0_LEN, 24
TAIL_AT, TAIL_LEN = FFN_AT + (N_SLAB - 1) * FFN_LEN, 8
N_CHUNKS = TAIL_AT + TAIL_LEN
YA_KTS = (2, 1, 1)
YB_KTS = (2, 2, 2, 1, 1)
MERGE0_KTS = (2,) * 16 + YA_KTS + YB_KTS
MERGE_KTS = (2,) * 24 + YA_KTS + YB_KTS


def build(nc, x, w_in, w_out_a, w_out_b, w_out, w_gate, w_up, w_down, g_mix, g_ffn, g_final,
          rel_bias, onehot, out, bias_rows):
    f32, f32r = mybir.dt.float32, mybir.dt.float32r
    ACT, ALU, AX = mybir.ActivationFunctionType, mybir.AluOpType, mybir.AxisListType
    w_in, w_out_a, w_out_b, w_out = w_in[0], w_out_a[0], w_out_b[0], w_out[0]
    w_gate, w_up, w_down = w_gate[0], w_up[0], w_down[0]

    ctx = ExitStack()
    with ctx:
        def sb(name, shape, dt=f32):
            return ctx.enter_context(nc.sbuf_tensor(name, shape, dt))

        def sem(name):
            return ctx.enter_context(nc.semaphore(name))

        xs = sb("xs", [P, BLK, D])
        h_hi = sb("h_hi", [P, KT, SEQ], f32r)
        h_lo = sb("h_lo", [P, KT, SEQ], f32r)
        raw = sb("raw", [P, RING, 2, NC_])
        w_hi = sb("w_hi", [P, RING, 2, NC_], f32r)
        w_lo = sb("w_lo", [P, RING, 2, NC_], f32r)
        bias = sb("bias", [P, N_HEADS, SKEW])
        u = sb("u", [P, N_QUAD, BLK, QW])
        y_hi = sb("y_hi", [P, 3 * QUAD, SEQ], f32r)
        y_lo = sb("y_lo", [P, 3 * QUAD, SEQ], f32r)
        slab_hi = sb("slab_hi", [P, QUAD, SEQ], f32r)
        slab_lo = sb("slab_lo", [P, QUAD, SEQ], f32r)
        stage = sb("stage", [P, BLK, QW])
        qk = sb("qk", [P, 2, QUAD, SEQ])
        v = sb("v", [P, BLK, QW])
        att = sb("att", [P, 6, SKEW])
        score = [att[:, j, :] for j in range(2)]
        prob = [att[:, 2 + j, :] for j in range(2)]
        prob_t = [att[:, 4 + j, :] for j in range(2)]
        ident = sb("ident", [P, P])
        g_rows = sb("g_rows", [2 * KT, P])
        g_cols = sb("g_cols", [P, 2 * KT])
        rel = sb("rel", [BUCKETS + 1, N_HEADS])
        neg_max = sb("neg_max", [P, N_QUAD, BLK * QUAD])
        denom = sb("denom", [P, N_QUAD, BLK * QUAD])
        mix = sb("mix", [P, 8, BLK * QUAD])
        sq = sb("sq", [P, BLK, N_OUT])
        norm = sb("norm", [P, 8, BLK])
        top = sb("top", [P, BLK, 8])
        w_idx = sb("w_idx", [P, BLK, N_IDX])
        flat_u = u[:].rearrange("p a b n -> p (a b n)")
        xn = flat_u[:, 0:BLK * D].rearrange("p (b n) -> p b n", b=BLK)
        qi_t = flat_u[:, 0:2048].rearrange("p (t s) -> p t s", t=8)
        ki_t = flat_u[:, 2048:2304]
        ki_twice = flat_u[:, 2304:2560].rearrange("p (b n) -> p b n", b=BLK)
        relu = [flat_u[:, 2560 + SKEW * j:2560 + SKEW * (j + 1)] for j in range(2)]
        idx_score = flat_u[:, BLK * D:BLK * D + SKEW]
        idx_left = flat_u[:, BLK * D + SKEW:BLK * D + 2 * SKEW]
        hot = qk[0:BUCKETS + 1].rearrange("p a j s -> p (a j s)")[:, 0:4 * SKEW] \
            .rearrange("p (g m) -> p g m", g=4)
        rows_sb = att[0:8, 0:4, :]
        sig_a, sig_b = [qk[:, i, :, :].rearrange("p j s -> p (j s)")
                        .rearrange("p (b n) -> p b n", b=BLK) for i in range(2)]
        silu = sig_a
        g_last = bias[:].rearrange("p h m -> p (h m)")[:, 0:D]

        acc = [[ctx.enter_context(nc.psum_tensor(f"acc{s}{b}", [P, NC_], f32)) for b in range(BLK)]
               for s in range(2)]
        tp = [ctx.enter_context(nc.psum_tensor(f"tp{b}", [P, NC_], f32)) for b in range(2)]
        pt = ctx.enter_context(nc.psum_tensor("pt", [P, NC_], f32))
        po = ctx.enter_context(nc.psum_tensor("po", [P, NC_], f32))
        four = [tp[0], tp[1], pt, po]
        dots = [pt, po]

        x_loaded = [sem(f"x_loaded{b}") for b in range(BLK)]
        g_loaded, hot_loaded, rel_loaded, g_last_loaded = sem("g_loaded"), sem("hot_loaded"), sem("rel_loaded"), sem("g_last_loaded")
        ident_zero, ident_made, rel_masked, idx_zero = sem("ident_zero"), sem("ident_made"), sem("rel_masked"), sem("idx_zero")
        bias_rows_made, bias_rows_out, bias_rows_stored, bias_loaded, bias_chosen, bias_step = sem("bias_rows_made"), sem("bias_rows_out"), sem("bias_rows_stored"), sem("bias_loaded"), sem("bias_chosen"), sem("bias_step")
        g_turned, g_out = sem("g_turned"), sem("g_out")
        squares, mean_made, root_made, scale_made, xn_made, norm_step = sem("squares"), sem("mean_made"), sem("root_made"), sem("scale_made"), sem("xn_made"), sem("norm_step")
        h_turned, h_hi_made, h_made = sem("h_turned"), sem("h_hi_made"), sem("h_made")
        raw_loaded = [sem(f"raw_loaded{s}") for s in range(RING)]
        hi_made, lo_made, chunk_used = sem("hi_made"), sem("lo_made"), sem("chunk_used")
        stage_made, stage_turned = sem("stage_made"), sem("stage_turned")
        ki_made, w_idx_made, ki_turned, ki_t_made, qi_t_made = sem("ki_made"), sem("w_idx_made"), sem("ki_turned"), sem("ki_t_made"), sem("qi_t_made")
        dots_made, relu_made, idx_added, top_step = sem("dots_made"), sem("relu_made"), sem("idx_added"), sem("top_step")
        qk_made, v_made = sem("qk_made"), sem("v_made")
        scored, biased, max_made, exp_made = sem("scored"), sem("biased"), sem("max_made"), sem("exp_made")
        prob_turned, prob_t_made, pv_made, u_made = sem("prob_turned"), sem("prob_t_made"), sem("pv_made"), sem("u_made")
        mix_step, mix_in, mix_exp = sem("mix_step"), sem("mix_in"), sem("mix_exp")
        part_hi, y_made, slab_made = sem("part_hi"), sem("y_made"), sem("slab_made")
        sig_made, gated_a, gated_b, merged = sem("sig_made"), sem("gated_a"), sem("gated_b"), sem("merged")
        silu_made, swiglu_made, x_added = sem("silu_made"), sem("swiglu_made"), sem("x_added")
        out_made, out_stored = sem("out_made"), sem("out_stored")

        FILL_QI = (0, 1)
        FILL_Q0, FILL_K0 = 2, 3
        FILL_Y = 2 + 2 * N_QUAD
        FILL_SLAB = FILL_Y + 3

        block = ctx.enter_context(nc.Block())

        @block.sync
        def _(sp):
            def load(at, t, src, turn=0):
                slot, c = t % RING, at + t
                if not (isinstance(at, int) and c < RING):
                    sp.wait_ge(lo_made, c - RING + 1)
                kts, width = src.shape[0] // P, src.shape[1]
                sp.dma_start(raw[:, slot, 0:kts, 0:width], src.rearrange("(t p) n -> p t n", p=P)) \
                    .then_inc(raw_loaded[slot], 16)

            def column(at, t0, w, col, width=NC_):
                for k in range(KT // 2):
                    load(at, t0 + k, w[2 * k * P:2 * (k + 1) * P, bass.ds(col, width)])

            def row_slab(at, t0, w, row):
                for n in range(N_OUT):
                    for k in range(2):
                        load(at, t0 + 2 * n + k, w[bass.ds(row + 2 * k * P, 2 * P), n * NC_:(n + 1) * NC_])

            def outs(at, t0, col):
                t = t0
                for w, kts in ((w_out_a, YA_KTS), (w_out_b, YB_KTS)):
                    row = 0
                    for k in kts:
                        load(at, t, w[row:row + k * P, bass.ds(col, NC_)])
                        row, t = row + k * P, t + 1

            column(IDX_AT, 0, w_in, COL_KI, KIW)
            column(IDX_AT, 8, w_in, COL_QI)
            column(IDX_AT, 16, w_in, COL_QI + NC_)
            with sp.Fori(0, N_GROUP_A) as i:
                for n, col in enumerate((COL_Q_A, COL_K_A, COL_V_A)):
                    column(QUAD_AT + QUAD_LEN * i, 8 * n, w_in, col + QW * i)
            with sp.Fori(0, N_QUAD_B) as i:
                for n, col in enumerate((COL_Q_B, COL_K_B, COL_V_B)):
                    column(QUAD_AT + N_GROUP_A * QUAD_LEN + QUAD_LEN * i, 8 * n, w_in, col + QW * i)
            column(MERGE0_AT, 0, w_in, COL_GA)
            column(MERGE0_AT, 8, w_in, COL_GB)
            outs(MERGE0_AT, 16, 0)
            with sp.Fori(0, N_OUT - 1) as n:
                at = MERGE_AT + MERGE_LEN * n
                column(at, 0, w_in, COL_GA + NC_ + NC_ * n)
                row_slab(at, 8, w_out, NC_ * n)
                column(at, 16, w_in, COL_GB + NC_ + NC_ * n)
                outs(at, 24, NC_ + NC_ * n)
            row_slab(WOUT_AT, 0, w_out, (N_OUT - 1) * NC_)
            column(FFN0_AT, 0, w_gate, 0)
            column(FFN0_AT, 8, w_up, 0)
            with sp.Fori(1, N_SLAB) as i:
                at = (FFN_AT - FFN_LEN) + FFN_LEN * i
                column(at, 0, w_gate, NC_ * i)
                row_slab(at, 8, w_down, NC_ * i - NC_)
                column(at, 16, w_up, NC_ * i)
            row_slab(TAIL_AT, 0, w_down, (N_SLAB - 1) * NC_)
            for b in range(BLK):
                for s in range(2):
                    sp.wait_ge(out_made, 2 * b + s + 1)
                    cols = slice(s * D // 2, (s + 1) * D // 2)
                    sp.dma_start(out[0, b * P:(b + 1) * P, cols], xs[:, b, cols]).then_inc(out_stored, 16)
            sp.wait_ge(out_stored, 16 * 2 * BLK)

        @block.gpsimd
        def _(pool):
            pool.dma_start(hot, onehot).then_inc(hot_loaded, 16)
            pool.dma_start(rel[0:BUCKETS, :], rel_bias).then_inc(rel_loaded, 16)
            pool.memset(rel[BUCKETS:BUCKETS + 1, :], NEG).then_inc(rel_masked, 1)
            pool.wait_ge(rel_masked, 1)
            pool.memset(ident[:], 0.0).then_inc(ident_zero, 1)
            pool.wait_ge(ident_zero, 1)
            pool.affine_select(out=ident[:], in_=ident[:], compare_op=ALU.not_equal, fill=1.0, base=0,
                               pattern=[[-1, P]], channel_multiplier=1).then_inc(ident_made, 1)
            pool.memset(idx_score, 0.0).then_inc(idx_zero, 1)
            pool.wait_ge(idx_zero, 1)
            pool.affine_select(out=idx_score[:, 0:P], in_=idx_score[:, 0:P], compare_op=ALU.is_ge, fill=NEG,
                               base=0, pattern=[[-1, P]], channel_multiplier=1).then_inc(idx_zero, 1)
            pool.affine_select(out=idx_score[:, P:SKEW], in_=idx_score[:, P:SKEW], compare_op=ALU.is_ge,
                               fill=NEG, base=P, pattern=[[-1, SEQ]], channel_multiplier=1).then_inc(idx_zero, 1)
            for g in range(4):
                n = 4 if g < 3 else 8
                pool.wait_ge(bias_rows_out, g + 1)
                pool.dma_start(bias_rows[4 * g:4 * g + n].rearrange("h (q m) -> h q m", q=P)[:, :, 0:SKEW],
                               rows_sb[0:n, g, :].unsqueeze(1).to_broadcast([n, P, SKEW])) \
                    .then_inc(bias_rows_stored, 16)
            pool.wait_ge(bias_rows_stored, 4 * 16)
            for a in range(N_QUAD):
                skewed = bias_rows[4 * a:4 * a + QUAD, 0:P * SKEW].rearrange("h (q m) -> q h m", q=P)
                for lo, width, at in ((P, P, 0), (0, SEQ, P)):
                    src = bass.AP(skewed.tensor, skewed.offset + P - 1 + lo, [*skewed.ap[:2], [1, width]])
                    pool.dma_start(bias[:, 4 * a:4 * a + QUAD, at:at + width], src).then_inc(bias_loaded, 16)
            pool.wait_ge(bias_loaded, 2 * N_QUAD * 16)
            pool.wait_ge(top_step, 4 * TOPK // 8)
            pool.tensor_scalar(idx_left, idx_left, TAKEN / 2, NEG, ALU.is_gt, ALU.mult).then_inc(bias_step, 1)
            pool.wait_ge(bias_step, 1)
            for h in range(N_GROUP_A * QUAD, N_HEADS):
                pool.tensor_tensor(bias[:, h, :], bias[:, h, :], idx_left, ALU.add).then_inc(bias_chosen, 1)
            pool.wait_ge(biased, N_HEADS)
            pool.dma_start(g_last, g_final.partition_broadcast(P)).then_inc(g_last_loaded, 16)

        @block.scalar
        def _(act):
            def hi(at, t, turn, kts=2, width=NC_):
                slot = t % RING
                act.wait_ge(raw_loaded[slot], 16 * (turn + t // RING + 1))
                if not (isinstance(at, int) and at + t < RING):
                    act.wait_ge(chunk_used, at + t - RING + 1)
                act.activation(w_hi[:, slot, 0:kts, 0:width], raw[:, slot, 0:kts, 0:width], ACT.Copy) \
                    .then_inc(hi_made, 1)

            def copy_stage(last_chunk, s, fill):
                act.wait_ge(chunk_used, last_chunk + 1)
                act.wait_ge(stage_turned, fill)
                act.activation(stage[:, 0, :], acc[s][0][:], ACT.Copy).then_inc(stage_made, 1)

            def copy_turned(dst, fill, done):
                act.wait_ge(stage_turned, fill + 1)
                act.activation(dst[:, :, 0:P], tp[0][:].rearrange("p (j s) -> p j s", j=QUAD), ACT.Copy) \
                    .then_inc(done, 1)

            def hi_turned(dst, fill):
                act.wait_ge(stage_turned, fill + 1)
                for b in range(BLK):
                    act.activation(dst[:, :, b * P:(b + 1) * P], tp[b][:].rearrange("p (j s) -> p j s", j=QUAD),
                                   ACT.Copy).then_inc(part_hi, 1)

            def exps(a, j):
                act.wait_ge(max_made, 8 * a + 2 * j + 2)
                if j >= 2:
                    act.wait_ge(prob_turned, 4 * a + j - 1)
                for b, cols in ((0, slice(0, P)), (1, slice(P, SKEW))):
                    i = b * QUAD + j
                    act.activation(prob[j % 2][:, cols], score[j % 2][:, cols], ACT.Exp,
                                   bias=neg_max[:, a, i:i + 1], accum_out=denom[:, a, i:i + 1]) \
                        .then_inc(exp_made, 1)

            def copy_prob(a, j):
                act.wait_ge(prob_turned, 4 * a + j + 1)
                if j >= 2:
                    act.wait_ge(pv_made, 4 * a + j - 1)
                act.activation(prob_t[j % 2], pt[:, 0:SKEW], ACT.Copy).then_inc(prob_t_made, 1)

            def attend(a, t):
                if t in (-1, 0, 2, 4):
                    exps(a, (-1, 0, 2, 4).index(t))
                if t in (1, 3, 5, 7):
                    copy_prob(a, (1, 3, 5, 7).index(t))

            def quad(at, i, t):
                if t == 7:
                    copy_stage(at + 7, 1, FILL_Q0 + 2 * i)
                if t == 10:
                    copy_turned(qk[:, 0], FILL_Q0 + 2 * i, qk_made)
                if t == 15:
                    copy_stage(at + 15, 0, FILL_K0 + 2 * i)
                if t == 18:
                    copy_turned(qk[:, 1], FILL_K0 + 2 * i, qk_made)
                if t == 23:
                    act.wait_ge(chunk_used, at + 24)
                    act.activation(v[:, 0, :], acc[1][0][:], ACT.Copy).then_inc(v_made, 1)

            def gates(at, t, s, dst, before):
                act.wait_ge(chunk_used, at + t + 1)
                if before is not None:
                    act.wait_ge(*before)
                for b in range(BLK):
                    act.activation(dst[:, b, :], acc[s][b][:], ACT.Sigmoid).then_inc(sig_made, 1)

            def square_part(added, n):
                act.wait_ge(x_added, added)
                for b in range(BLK):
                    act.activation(xn[:, b, n * NC_:(n + 1) * NC_], xs[:, b, n * NC_:(n + 1) * NC_], ACT.Square,
                                   accum_out=sq[:, b, n:n + 1]).then_inc(squares, 1)

            def normed_split(which):
                act.wait_ge(mean_made, which + 1)
                act.activation(norm[:, 1, :], norm[:, 0, :], ACT.Sqrt).then_inc(root_made, 1)
                act.wait_ge(scale_made, which + 1)
                act.activation(xn[:, 0, :], xs[:, 0, :], ACT.Copy, scale=norm[:, 6, 0:1]).then_inc(xn_made, 1)
                if which == 0:
                    act.wait_ge(g_out, 1)
                for k in range(KT):
                    act.wait_ge(h_turned, KT * which + k // 2 * 2 + 2)
                    act.activation(h_hi[:, k, :], four[k // 2 % 4][:, k % 2 * SEQ:(k % 2 + 1) * SEQ], ACT.Copy,
                                   scale=g_cols[:, KT * which + k:KT * which + k + 1]).then_inc(h_hi_made, 1)

            for b in range(BLK):
                act.dma_start(xs[:, b, :], x[0, b * P:(b + 1) * P, :]).then_inc(x_loaded[b], 16)
            act.dma_start(g_rows[0:KT, :], g_mix.rearrange("a (k p) -> (a k) p", p=P)).then_inc(g_loaded, 16)
            act.dma_start(g_rows[KT:2 * KT, :], g_ffn.rearrange("a (k p) -> (a k) p", p=P)).then_inc(g_loaded, 16)
            act.wait_ge(x_loaded[0], 16)
            act.activation(xn[:, 0, :], xs[:, 0, :], ACT.Square, accum_out=sq[:, 0, 0:1]).then_inc(squares, 1)
            for t in range(AHEAD):
                hi(IDX_AT, t, 0, width=KIW)
            normed_split(0)

            for t in range(IDX_LEN):
                hi(IDX_AT, t + AHEAD, 0, width=KIW if t + AHEAD < 8 else NC_)
                if t == 9:
                    act.wait_ge(ki_turned, 1)
                    act.activation(ki_t[:, 0:P], tp[0][:, 0:P], ACT.Copy).then_inc(ki_t_made, 1)
                if t == 15:
                    copy_stage(IDX_AT + 15, 1, FILL_QI[0])
                if t == 17:
                    copy_turned(qi_t[:, 0:4], FILL_QI[0], qi_t_made)
                if t == 23:
                    copy_stage(IDX_AT + 23, 0, FILL_QI[1])

            for t in range(QUAD_LEN):
                hi(QUAD_AT, t + AHEAD, QUAD_AT // RING)
                if t == 1:
                    copy_turned(qi_t[:, 4:8], FILL_QI[1], qi_t_made)
                if 2 <= t < 2 + N_IDX:
                    h = t - 2
                    act.wait_ge(dots_made, h + 1)
                    if h >= 2:
                        act.wait_ge(idx_added, 2 * (h - 1))
                    act.activation(relu[h % 2], dots[h % 2][:, 0:SKEW], ACT.Relu).then_inc(relu_made, 1)
                quad(QUAD_AT, 0, t)

            with act.Fori(1, N_QUAD) as i:
                at = QUAD_AT + QUAD_LEN * i
                attend(i - 1, -1)
                for t in range(QUAD_LEN):
                    hi(at, t + AHEAD, QUAD_AT // RING + QUAD_LEN // RING * i)
                    attend(i - 1, t)
                    quad(at, i, t)

            attend(N_QUAD - 1, -1)
            for t in range(MERGE0_LEN):
                nxt = t + AHEAD
                hi(MERGE0_AT, nxt, MERGE0_AT // RING, MERGE0_KTS[nxt] if nxt < MERGE0_LEN else 2)
                attend(N_QUAD - 1, t)
                if t == 8:
                    act.wait_ge(mix_in, 1)
                    act.activation(mix[:, 4:7, :], mix[:, 1:4, :], ACT.Exp).then_inc(mix_exp, 1)
                if t == 9:
                    gates(MERGE0_AT, 7, 0, sig_a, (scored, N_HEADS))
                if t in (12, 14, 16):
                    n = (t - 12) // 2
                    hi_turned(y_hi[:, QUAD * n:QUAD * (n + 1)], FILL_Y + n)
                if t == 15:
                    gates(MERGE0_AT, 15, 1, sig_b, None)
            with act.Fori(1, N_OUT) as n:
                at = (MERGE_AT - MERGE_LEN) + MERGE_LEN * n
                turn = (MERGE_AT - MERGE_LEN) // RING + MERGE_LEN // RING * n
                for t in range(MERGE_LEN):
                    nxt = t + AHEAD
                    hi(at, nxt, turn, MERGE_KTS[nxt] if nxt < MERGE_LEN else 2)
                    if t == 2:
                        hi_turned(slab_hi[:], FILL_SLAB - 1 + n)
                    if t == 7:
                        gates(at, 7, 0, sig_a, (gated_a, 2 * n))
                    if t == 23:
                        gates(at, 23, 1, sig_b, (merged, n))
            hi_turned(slab_hi[:], FILL_SLAB + N_OUT - 1)
            for t in range(WOUT_LEN):
                hi(WOUT_AT, t + AHEAD, WOUT_AT // RING)
                if t % 2:
                    square_part(2 * N_OUT * (N_OUT - 1) + t + 1, t // 2)
            normed_split(1)

            for t in range(FFN0_LEN):
                hi(FFN0_AT, t + AHEAD, FFN0_AT // RING)
                if t == 7:
                    act.wait_ge(chunk_used, FFN0_AT + 8)
                    for b in range(BLK):
                        act.activation(silu[:, b, :], acc[0][b][:], ACT.Silu).then_inc(silu_made, 1)
            with act.Fori(1, N_SLAB) as i:
                at = (FFN_AT - FFN_LEN) + FFN_LEN * i
                for t in range(FFN_LEN):
                    hi(at, t + AHEAD, (FFN_AT - FFN_LEN) // RING + FFN_LEN // RING * i)
                    if t == 2:
                        hi_turned(slab_hi[:], FILL_SLAB + N_OUT - 1 + i)
                    if t == 7:
                        act.wait_ge(chunk_used, at + 8)
                        for b in range(BLK):
                            act.activation(silu[:, b, :], acc[0][b][:], ACT.Silu).then_inc(silu_made, 1)
            hi_turned(slab_hi[:], FILL_SLAB + N_OUT + N_SLAB - 1)
            for t in range(TAIL_LEN):
                if t + AHEAD < TAIL_LEN:
                    hi(TAIL_AT, t + AHEAD, TAIL_AT // RING)
                if t % 2:
                    square_part(2 * N_OUT * (N_OUT + N_SLAB - 1) + t + 1, t // 2)
            act.wait_ge(mean_made, 3)
            act.activation(norm[:, 1, :], norm[:, 0, :], ACT.Sqrt).then_inc(root_made, 1)

        @block.vector
        def _(dve):
            class Chain:

                def __init__(self, s):
                    self.s, self.n = s, 0

                def then(self, ins):
                    self.n += 1
                    ins.then_inc(self.s, 1)
                    dve.wait_ge(self.s, self.n)

            def lo(at, t, kts=2, width=NC_):
                slot = t % RING
                dve.wait_ge(hi_made, at + t + 1)
                dve.tensor_tensor(w_lo[:, slot, 0:kts, 0:width], raw[:, slot, 0:kts, 0:width],
                                  w_hi[:, slot, 0:kts, 0:width].bitcast(f32), ALU.subtract).then_inc(lo_made, 1)

            def copy_stage(last_chunk, s, fill):
                dve.wait_ge(chunk_used, last_chunk + 1)
                dve.wait_ge(stage_turned, fill)
                dve.tensor_copy(stage[:, 1, :], acc[s][1][:]).then_inc(stage_made, 1)

            def copy_turned(dst, fill, done):
                dve.wait_ge(stage_turned, fill + 1)
                dve.tensor_copy(dst[:, :, P:SEQ], tp[1][:].rearrange("p (j s) -> p j s", j=QUAD)).then_inc(done, 1)

            def lo_turned(dst, of, fill, done):
                for b in range(BLK):
                    dve.wait_ge(part_hi, 2 * (fill - FILL_Y) + b + 1)
                    cols = slice(b * P, (b + 1) * P)
                    dve.tensor_tensor(dst[:, :, cols], tp[b][:].rearrange("p (j s) -> p j s", j=QUAD),
                                      of[:, :, cols].bitcast(f32), ALU.subtract).then_inc(done, 1)

            def scores(a, j):
                dve.wait_ge(scored, 4 * a + j + 1)
                if j >= 2:
                    dve.wait_ge(exp_made, 8 * a + 2 * (j - 1))
                dve.scalar_tensor_tensor(out=score[j % 2], in0=tp[j % 2][:, 0:SKEW], scalar=HD ** -0.5,
                                         in1=bias[:, 4 * a + j, :], op0=ALU.mult, op1=ALU.add).then_inc(biased, 1)
                dve.wait_ge(biased, 4 * a + j + 1)
                for b, cols in ((0, slice(0, P)), (1, slice(P, SKEW))):
                    i = b * QUAD + j
                    dve.tensor_reduce(neg_max[:, a, i:i + 1], score[j % 2][:, cols], AX.X, ALU.max,
                                      negate=True).then_inc(max_made, 1)

            def copy_out(a, j):
                dve.wait_ge(pv_made, 4 * a + j + 1)
                dve.tensor_copy(u[:, a, :, j * HD:(j + 1) * HD],
                                po[:, 0:SEQ].rearrange("p (b d) -> p b d", b=BLK)).then_inc(u_made, 1)

            def attend(a, t):
                if t == -1:
                    scores(a, 0)
                    scores(a, 1)
                if t in (2, 4):
                    scores(a, 2 + (t - 2) // 2)
                if t in (3, 5, 7, 9):
                    copy_out(a, (t - 3) // 2)

            def quad(at, i, t):
                if t == 7:
                    copy_stage(at + 7, 1, FILL_Q0 + 2 * i)
                if t == 10:
                    copy_turned(qk[:, 0], FILL_Q0 + 2 * i, qk_made)
                if t == 15:
                    copy_stage(at + 15, 0, FILL_K0 + 2 * i)
                if t == 18:
                    copy_turned(qk[:, 1], FILL_K0 + 2 * i, qk_made)
                if t == 23:
                    dve.wait_ge(chunk_used, at + 24)
                    dve.tensor_copy(v[:, 1, :], acc[1][1][:]).then_inc(v_made, 1)

            def add_x(at, t, s, n):
                dve.wait_ge(chunk_used, at + t + 1)
                for b in range(BLK):
                    cols = slice(n * NC_, (n + 1) * NC_)
                    dve.tensor_tensor(xs[:, b, cols], acc[s][b][:], xs[:, b, cols], ALU.add).then_inc(x_added, 1)

            def gate_a(at, t, n):
                dve.wait_ge(chunk_used, at + t + 1)
                dve.wait_ge(sig_made, 4 * n + 2)
                dve.wait_ge(stage_turned, FILL_SLAB + n)
                for b in range(BLK):
                    dve.tensor_tensor(stage[:, b, :], acc[0][b][:], sig_a[:, b, :], ALU.mult).then_inc(gated_a, 1)

            def gate_b(at, t, n):
                dve.wait_ge(chunk_used, at + t + 1)
                dve.wait_ge(sig_made, 4 * n + 4)
                for b in range(BLK):
                    dve.tensor_tensor(sig_b[:, b, :], acc[1][b][:], sig_b[:, b, :], ALU.mult).then_inc(gated_b, 1)
                dve.wait_ge(gated_a, 2 * n + 2)
                dve.wait_ge(gated_b, 2 * n + 2)
                dve.tensor_tensor(stage[:], stage[:], sig_b, ALU.add).then_inc(merged, 1)

            norm_chain = Chain(norm_step)

            def scale_rows(which, parts):
                dve.wait_ge(squares, (1, 1 + 2 * N_OUT, 1 + 4 * N_OUT)[which])
                if parts > 1:
                    norm_chain.then(dve.tensor_reduce(norm[:, 2, :], sq[:], AX.X, ALU.add))
                else:
                    norm_chain.then(dve.tensor_copy(norm[:, 2, :], sq[:, :, 0]))
                dve.tensor_scalar(norm[:, 0, :], norm[:, 2, :], 1.0 / D, EPS, ALU.mult, ALU.add).then_inc(mean_made, 1)
                dve.wait_ge(root_made, which + 1)
                norm_chain.then(dve.reciprocal(norm[:, 3, :], norm[:, 1, :]))
                norm_chain.then(dve.tensor_tensor(norm[:, 4, :], norm[:, 3, :], norm[:, 3, :], ALU.mult))
                norm_chain.then(dve.tensor_tensor(norm[:, 5, :], norm[:, 4, :], norm[:, 0, :], ALU.mult))
                norm_chain.then(dve.tensor_scalar(norm[:, 7, :], norm[:, 5, :], -0.5, 1.5, ALU.mult, ALU.add))
                dve.tensor_tensor(norm[:, 6, :], norm[:, 3, :], norm[:, 7, :], ALU.mult).then_inc(scale_made, 1)
                dve.wait_ge(scale_made, which + 1)

            def normed_split(which):
                dve.tensor_scalar(xn[:, 1, :], xs[:, 1, :], norm[:, 6, 1:2], None, ALU.mult).then_inc(xn_made, 1)
                for k in range(KT):
                    dve.wait_ge(h_hi_made, KT * which + k // 2 * 2 + 2)
                    dve.scalar_tensor_tensor(out=h_lo[:, k, :], in0=four[k // 2 % 4][:, k % 2 * SEQ:(k % 2 + 1) * SEQ],
                                             scalar=g_cols[:, KT * which + k:KT * which + k + 1],
                                             in1=h_hi[:, k, :].bitcast(f32), op0=ALU.mult,
                                             op1=ALU.subtract).then_inc(h_made, 1)

            for g in range(4):
                n = 4 if g < 3 else 8
                dve.wait_ge(bias_rows_made, g + 1)
                dve.tensor_copy(rows_sb[0:n, g, :], four[g][0:n, 0:SKEW]).then_inc(bias_rows_out, 1)
            dve.wait_ge(g_turned, 1)
            dve.tensor_copy(g_cols[:], acc[0][0][:, 0:2 * KT]).then_inc(g_out, 1)
            dve.wait_ge(x_loaded[1], 16)
            norm_chain.then(dve.tensor_tensor_reduce(out=xn[:, 1, :], in0=xs[:, 1, :], in1=xs[:, 1, :], scale=1.0,
                                                     scalar=0.0, op0=ALU.mult, op1=ALU.add,
                                                     accum_out=sq[:, 1, 0:1]))
            for t in range(AHEAD):
                lo(IDX_AT, t, width=KIW)
            scale_rows(0, 1)
            dve.wait_ge(g_out, 1)
            normed_split(0)

            for t in range(IDX_LEN):
                lo(IDX_AT, t + AHEAD, width=KIW if t + AHEAD < 8 else NC_)
                if t == 7:
                    dve.wait_ge(chunk_used, IDX_AT + 8)
                    for b in range(BLK):
                        dve.tensor_copy(ki_twice[:, b, 0:IDX], acc[0][b][:, 0:IDX]).then_inc(ki_made, 1)
                        dve.tensor_copy(ki_twice[:, b, IDX:P], acc[0][b][:, 0:IDX]).then_inc(ki_made, 1)
                        dve.tensor_scalar(w_idx[:, b, :], acc[0][b][:, IDX:KIW], (IDX ** -0.5) * (N_IDX ** -0.5),
                                          None, ALU.mult).then_inc(w_idx_made, 1)
                if t == 9:
                    dve.wait_ge(ki_turned, 1)
                    dve.tensor_copy(ki_t[:, P:SEQ], tp[1][:, 0:P]).then_inc(ki_t_made, 1)
                if t == 15:
                    copy_stage(IDX_AT + 15, 1, FILL_QI[0])
                if t == 17:
                    copy_turned(qi_t[:, 0:4], FILL_QI[0], qi_t_made)
                if t == 23:
                    copy_stage(IDX_AT + 23, 0, FILL_QI[1])

            top_chain = Chain(top_step)
            halves = ((0, slice(0, P)), (1, slice(P, SKEW)))

            def top_round(r):
                left = idx_score if r == 0 else idx_left
                for b, cols in halves:
                    ins = dve.max(top[:, b, :], left[:, cols])
                    top_chain.n += 1
                    ins.then_inc(top_step, 1)
                dve.wait_ge(top_step, top_chain.n)
                for b, cols in halves:
                    ins = dve.match_replace(out=idx_left[:, cols], in_to_replace=top[:, b, :],
                                            in_values=left[:, cols], imm_value=TAKEN)
                    top_chain.n += 1
                    ins.then_inc(top_step, 1)
                dve.wait_ge(top_step, top_chain.n)

            for t in range(QUAD_LEN):
                lo(QUAD_AT, t + AHEAD)
                if t == 1:
                    copy_turned(qi_t[:, 4:8], FILL_QI[1], qi_t_made)
                if 2 <= t < 2 + N_IDX:
                    h = t - 2
                    if h == 0:
                        dve.wait_ge(idx_zero, 3)
                    else:
                        dve.wait_ge(idx_added, 2 * h)
                    dve.wait_ge(relu_made, h + 1)
                    for b, cols in halves:
                        dve.scalar_tensor_tensor(out=idx_score[:, cols], in0=relu[h % 2][:, cols],
                                                 scalar=w_idx[:, b, h:h + 1], in1=idx_score[:, cols],
                                                 op0=ALU.mult, op1=ALU.add).then_inc(idx_added, 1)
                quad(QUAD_AT, 0, t)
                if t == 18:
                    dve.wait_ge(idx_added, 2 * N_IDX)
                if t >= 18:
                    top_round(t - 18)
                if t == 22:
                    top_round(6)
            top_round(7)

            def quad_pass(i):
                at = QUAD_AT + QUAD_LEN * i
                attend(i - 1, -1)
                for t in range(QUAD_LEN):
                    lo(at, t + AHEAD)
                    attend(i - 1, t)
                    quad(at, i, t)

            dve.wait_ge(bias_loaded, 2 * N_QUAD * 16)
            with dve.Fori(1, N_GROUP_A + 1) as i:
                quad_pass(i)
            dve.wait_ge(bias_chosen, N_QUAD_B * QUAD)
            quad_pass(N_QUAD - 1)

            mix_chain = Chain(mix_step)

            def spread(weights):
                return weights.unsqueeze(2).to_broadcast([P, BLK * QUAD, HD])

            def heads(rows):
                return rows.rearrange("p b (j d) -> p (b j) d", j=QUAD)

            attend(N_QUAD - 1, -1)
            for t in range(MERGE0_LEN):
                nxt = t + AHEAD
                lo(MERGE0_AT, nxt, MERGE0_KTS[nxt] if nxt < MERGE0_LEN else 2)
                attend(N_QUAD - 1, t)
                if t == 6:
                    dve.wait_ge(u_made, 4 * N_GROUP_A)
                    mix_chain.then(dve.tensor_tensor(mix[:, 0, :], neg_max[:, 0, :], neg_max[:, 1, :], ALU.min))
                    mix_chain.then(dve.tensor_tensor(mix[:, 0, :], mix[:, 0, :], neg_max[:, 2, :], ALU.min))
                    for g in range(N_GROUP_A):
                        ins = dve.tensor_tensor(mix[:, 1 + g, :], mix[:, 0, :], neg_max[:, g, :], ALU.subtract)
                        if g < N_GROUP_A - 1:
                            mix_chain.then(ins)
                    ins.then_inc(mix_in, 1)
                if t == 8:
                    dve.wait_ge(mix_exp, 1)
                    mix_chain.then(dve.tensor_tensor(mix[:, 1:4, :], mix[:, 4:7, :], denom[:, 0:3, :], ALU.mult))
                    mix_chain.then(dve.tensor_tensor(mix[:, 0, :], mix[:, 1, :], mix[:, 2, :], ALU.add))
                    mix_chain.then(dve.tensor_tensor(mix[:, 0, :], mix[:, 0, :], mix[:, 3, :], ALU.add))
                    mix_chain.then(dve.reciprocal(mix[:, 7, :], mix[:, 0, :]))
                    for g in range(N_GROUP_A):
                        mix_chain.then(dve.tensor_tensor(mix[:, 4 + g, :], mix[:, 4 + g, :], mix[:, 7, :], ALU.mult))
                if t in (8, 9, 10):
                    g = t - 8
                    mix_chain.then(dve.tensor_tensor(heads(u[:, g]), heads(u[:, g]), spread(mix[:, 4 + g, :]), ALU.mult))
                if t == 10:
                    mix_chain.then(dve.tensor_tensor(u[:, 0], u[:, 0], u[:, 1], ALU.add))
                if t == 11:
                    dve.wait_ge(stage_turned, FILL_Y)
                    dve.tensor_tensor(stage[:], u[:, 0], u[:, 2], ALU.add).then_inc(stage_made, 2)
                    dve.wait_ge(u_made, N_HEADS)
                    mix_chain.then(dve.reciprocal(mix[:, 0:2, :], denom[:, 3:5, :]))
                if t == 12:
                    lo_turned(y_lo[:, 0:QUAD], y_hi[:, 0:QUAD], FILL_Y, y_made)
                if t in (12, 14):
                    n = (t - 12) // 2
                    dve.wait_ge(stage_turned, FILL_Y + 1 + n)
                    dve.tensor_tensor(heads(stage[:]), heads(u[:, 3 + n]), spread(mix[:, n, :]), ALU.mult) \
                        .then_inc(stage_made, 2)
                if t in (14, 16):
                    n = (t - 12) // 2
                    lo_turned(y_lo[:, QUAD * n:QUAD * (n + 1)], y_hi[:, QUAD * n:QUAD * (n + 1)], FILL_Y + n, y_made)
                if t == 18:
                    gate_a(MERGE0_AT, t, 0)
                if t == 23:
                    gate_b(MERGE0_AT, t, 0)
            with dve.Fori(1, N_OUT) as n:
                at = (MERGE_AT - MERGE_LEN) + MERGE_LEN * n
                for t in range(MERGE_LEN):
                    nxt = t + AHEAD
                    lo(at, nxt, MERGE_KTS[nxt] if nxt < MERGE_LEN else 2)
                    if t == 2:
                        lo_turned(slab_lo[:], slab_hi, FILL_SLAB - 1 + n, slab_made)
                    if t in (9, 11, 13, 15):
                        add_x(at, t, (t - 7) // 2 % 2, (t - 9) // 2)
                    if t == 26:
                        gate_a(at, t, n)
                    if t == 31:
                        gate_b(at, t, n)
            lo_turned(slab_lo[:], slab_hi, FILL_SLAB + N_OUT - 1, slab_made)
            for t in range(WOUT_LEN):
                lo(WOUT_AT, t + AHEAD)
                if t % 2:
                    add_x(WOUT_AT, t, t // 2 % 2, t // 2)
            scale_rows(1, N_OUT)
            normed_split(1)

            def swiglu(at, t, i):
                dve.wait_ge(chunk_used, at + t + 1)
                dve.wait_ge(silu_made, 2 * i + 2)
                dve.wait_ge(stage_turned, FILL_SLAB + N_OUT + i)
                for b in range(BLK):
                    dve.tensor_tensor(stage[:, b, :], acc[1][b][:], silu[:, b, :], ALU.mult).then_inc(swiglu_made, 1)

            for t in range(FFN0_LEN):
                lo(FFN0_AT, t + AHEAD)
                if t == 15:
                    swiglu(FFN0_AT, t, 0)
            with dve.Fori(1, N_SLAB) as i:
                at = (FFN_AT - FFN_LEN) + FFN_LEN * i
                for t in range(FFN_LEN):
                    lo(at, t + AHEAD)
                    if t == 2:
                        lo_turned(slab_lo[:], slab_hi, FILL_SLAB + N_OUT - 1 + i, slab_made)
                    if t in (9, 11, 13, 15):
                        add_x(at, t, (t - 7) // 2 % 2, (t - 9) // 2)
                    if t == 23:
                        swiglu(at, t, i)
            lo_turned(slab_lo[:], slab_hi, FILL_SLAB + N_OUT + N_SLAB - 1, slab_made)
            for t in range(TAIL_LEN):
                if t + AHEAD < TAIL_LEN:
                    lo(TAIL_AT, t + AHEAD)
                if t % 2:
                    add_x(TAIL_AT, t, t // 2 % 2, t // 2)
            scale_rows(2, N_OUT)
            dve.wait_ge(g_last_loaded, 16)
            for b in range(BLK):
                for s in range(2):
                    cols = slice(s * D // 2, (s + 1) * D // 2)
                    dve.scalar_tensor_tensor(out=xs[:, b, cols], in0=xs[:, b, cols], scalar=norm[:, 6, b:b + 1],
                                             in1=g_last[:, cols], op0=ALU.mult, op1=ALU.mult).then_inc(out_made, 1)

        @block.tensor
        def _(pe):
            def chunk(at, t, x_hi, x_lo, k0, s, first, last, kts=2, width=NC_):
                slot = t % RING
                pe.wait_ge(lo_made, at + t + 1)
                for k in range(kts):
                    for b in range(BLK):
                        rows = slice(b * P, (b + 1) * P)
                        dst = acc[s][b][:, 0:width]
                        a_hi, a_lo = x_hi[:, k0 + k, rows], x_lo[:, k0 + k, rows]
                        b_hi, b_lo = w_hi[:, slot, k, 0:width], w_lo[:, slot, k, 0:width]
                        pe.matmul(dst, a_hi, b_hi, start=first and k == 0, stop=False)
                        pe.matmul(dst, a_hi, b_lo, start=False, stop=False)
                        ins = pe.matmul(dst, a_lo, b_hi, start=False, stop=last and k == kts - 1)
                ins.then_inc(chunk_used, 1)

            def column_chunk(at, t, j, s, free, width=NC_, h_from=None):
                if j == 0:
                    for f in free:
                        pe.wait_ge(*f)
                if h_from is not None:
                    pe.wait_ge(h_made, h_from + 2 * j + 2)
                chunk(at, t, h_hi, h_lo, 2 * j, s, j == 0, j == KT // 2 - 1, width=width)

            def slab_chunk(at, t, j, s, free):
                if j % 2 == 0:
                    for f in free:
                        pe.wait_ge(*f)
                chunk(at, t, slab_hi, slab_lo, j % 2 * 2, s, j % 2 == 0, j % 2 == 1)

            def turn(made, free):
                pe.wait_ge(*made)
                for f in free:
                    pe.wait_ge(*f)
                for b in range(BLK):
                    for j in range(QUAD):
                        ins = pe.transpose(tp[b][:, j * P:(j + 1) * P], stage[:, b, j * P:(j + 1) * P], ident[:])
                ins.then_inc(stage_turned, 1)

            def qk_product(a, j):
                if j < 2:
                    pe.wait_ge(qk_made, 4 * a + 4)
                else:
                    pe.wait_ge(biased, 4 * a + j - 1)
                dst = tp[j % 2]
                pe.matmul(dst[:, 0:P], qk[:, 0, j, 0:P], qk[:, 1, j, 0:P], start=True, stop=True)
                pe.matmul(dst[:, P:SKEW], qk[:, 0, j, P:SEQ], qk[:, 1, j, :], start=True, stop=True) \
                    .then_inc(scored, 1)

            def prob_turn(a, j):
                pe.wait_ge(exp_made, 8 * a + 2 * j + 2)
                if j:
                    pe.wait_ge(prob_t_made, 4 * a + j)
                for n in range(3):
                    cols = slice(n * P, (n + 1) * P)
                    ins = pe.transpose(pt[:, cols], prob[j % 2][:, cols], ident[:])
                ins.then_inc(prob_turned, 1)

            def pv_product(a, j):
                pe.wait_ge(prob_t_made, 4 * a + j + 1)
                pe.wait_ge(v_made, 2 * a + 2)
                if j:
                    pe.wait_ge(u_made, 4 * a + j)
                cols = slice(j * HD, (j + 1) * HD)
                pe.matmul(po[:, 0:P], prob_t[j % 2][:, 0:P], v[:, 0, cols], start=True, stop=True)
                pe.matmul(po[:, P:SEQ], prob_t[j % 2][:, P:2 * P], v[:, 0, cols], start=True, stop=False)
                pe.matmul(po[:, P:SEQ], prob_t[j % 2][:, 2 * P:SKEW], v[:, 1, cols], start=False, stop=True) \
                    .then_inc(pv_made, 1)

            def attend(a, t):
                if t == -1:
                    qk_product(a, 0)
                    qk_product(a, 1)
                if t in (3, 5, 7, 9):
                    pv_product(a, (t - 3) // 2)
                if t in (1, 3, 5, 7):
                    prob_turn(a, (t - 1) // 2)
                if t in (2, 4):
                    qk_product(a, 2 + (t - 2) // 2)

            def quad_chunk(at, i, t, q_free, q_tp_free):
                if t < 8:
                    column_chunk(at, t, t, 1, q_free)
                elif t < 16:
                    column_chunk(at, t, t - 8, 0, [(stage_made, 4 * i + 4)])
                else:
                    column_chunk(at, t, t - 16, 1, [(stage_made, 4 * i + 6)])
                if t == 10:
                    turn((stage_made, 2 * (FILL_Q0 + 2 * i) + 2), q_tp_free)
                if t == 18:
                    turn((stage_made, 2 * (FILL_K0 + 2 * i) + 2), [(qk_made, 4 * i + 2)])

            def turn_normed(which, free):
                pe.wait_ge(xn_made, 2 * which + 2)
                for k in range(KT):
                    bank = four[k // 2 % 4]
                    if k % 2 == 0:
                        if k < 8:
                            pe.wait_ge(*free[k // 2])
                        else:
                            pe.wait_ge(h_made, KT * which + k - 6)
                    for b in range(BLK):
                        ins = pe.transpose(bank[:, k % 2 * SEQ + b * P:k % 2 * SEQ + (b + 1) * P],
                                           xn[:, b, k * P:(k + 1) * P], ident[:])
                    ins.then_inc(h_turned, 1)

            pe.wait_ge(hot_loaded, 16)
            pe.wait_ge(rel_loaded, 16)
            pe.wait_ge(rel_masked, 1)
            for g in range(4):
                n = 4 if g < 3 else 8
                pe.matmul(four[g][0:n, 0:SKEW], rel[:, 4 * g:4 * g + n], hot[:, g, :], start=True, stop=True) \
                    .then_inc(bias_rows_made, 1)
            pe.wait_ge(g_loaded, 32)
            pe.wait_ge(ident_made, 1)
            pe.transpose(acc[0][0][:, 0:2 * KT], g_rows[:], ident[0:2 * KT, 0:2 * KT]).then_inc(g_turned, 1)
            turn_normed(0, [(bias_rows_out, g + 1) for g in range(4)])

            for t in range(IDX_LEN):
                if t < 8:
                    column_chunk(IDX_AT, t, t, 0, [(g_out, 1)], width=KIW, h_from=0)
                elif t < 16:
                    column_chunk(IDX_AT, t, t - 8, 1, [])
                else:
                    column_chunk(IDX_AT, t, t - 16, 0, [(w_idx_made, 2)])
                if t == 9:
                    pe.wait_ge(ki_made, 4)
                    for b in range(BLK):
                        ins = pe.transpose(tp[b][:, 0:P], ki_twice[:, b, :], ident[:])
                    ins.then_inc(ki_turned, 1)
                if t == 17:
                    turn((stage_made, 2), [(ki_t_made, 2)])

            for t in range(QUAD_LEN):
                quad_chunk(QUAD_AT, 0, t, [(stage_made, 2)], [(qi_t_made, 4)])
                if t == 1:
                    turn((stage_made, 4), [(qi_t_made, 2)])
                if 2 <= t < 2 + N_IDX:
                    h = t - 2
                    pe.wait_ge(qi_t_made, 2 if h < 8 else 4)
                    if h >= 2:
                        pe.wait_ge(relu_made, h - 1)
                    half = slice(h % 2 * IDX, (h % 2 + 1) * IDX)
                    pe.matmul(dots[h % 2][:, 0:P], qi_t[half, h // 2, 0:P], ki_t[half, 0:P], start=True, stop=True)
                    pe.matmul(dots[h % 2][:, P:SKEW], qi_t[half, h // 2, P:SEQ], ki_t[half, :],
                              start=True, stop=True).then_inc(dots_made, 1)

            pe.wait_ge(relu_made, N_IDX)
            with pe.Fori(1, N_QUAD) as i:
                at = QUAD_AT + QUAD_LEN * i
                attend(i - 1, -1)
                for t in range(QUAD_LEN):
                    quad_chunk(at, i, t, [(v_made, 2 * i)], [(biased, 4 * i)])
                    attend(i - 1, t)

            def y_chunk(at, t, t0, s, kts, k0, free):
                j = t - t0
                if j == 0:
                    for f in free:
                        pe.wait_ge(*f)
                chunk(at, t, y_hi, y_lo, k0 + sum(kts[:j]), s, j == 0, j == len(kts) - 1, kts[j])

            attend(N_QUAD - 1, -1)
            for t in range(MERGE0_LEN):
                if t < 8:
                    column_chunk(MERGE0_AT, t, t, 0, [(stage_made, 2 * (FILL_K0 + 2 * N_QUAD - 1))])
                elif t < 16:
                    column_chunk(MERGE0_AT, t, t - 8, 1, [(v_made, 2 * N_QUAD)])
                elif t < 19:
                    y_chunk(MERGE0_AT, t, 16, 0, YA_KTS, 0, [(sig_made, 2), (y_made, 2)])
                else:
                    y_chunk(MERGE0_AT, t, 19, 1, YB_KTS, QUAD, [(sig_made, 4), (y_made, 6)])
                attend(N_QUAD - 1, t)
                if t == 12:
                    turn((stage_made, 2 * FILL_Y + 2), [(biased, N_HEADS)])
                if t in (14, 16):
                    n = (t - 12) // 2
                    turn((stage_made, 2 * (FILL_Y + n) + 2), [(y_made, 2 * n)])
            with pe.Fori(1, N_OUT) as n:
                at = (MERGE_AT - MERGE_LEN) + MERGE_LEN * n
                added = 2 * N_OUT * n - 2 * N_OUT
                w_free = ((gated_b, 2 * n), (sig_made, 4 * n + 2), (x_added, added + 2), (x_added, added + 4))
                for t in range(MERGE_LEN):
                    if t < 8:
                        column_chunk(at, t, t, 0, [(gated_a, 2 * n)])
                    elif t < 16:
                        if t == 8:
                            pe.wait_ge(slab_made, 2 * n)
                        slab_chunk(at, t, t - 8, (t - 6) // 2 % 2, [w_free[(t - 8) // 2]])
                    elif t < 24:
                        column_chunk(at, t, t - 16, 1, [(x_added, added + 6)])
                    elif t < 27:
                        y_chunk(at, t, 24, 0, YA_KTS, 0, [(x_added, added + 8)])
                    else:
                        y_chunk(at, t, 27, 1, YB_KTS, QUAD, [(sig_made, 4 * n + 4)])
                    if t == 2:
                        turn((merged, n), [(y_made, 6)])
            turn((merged, N_OUT), [(slab_made, 2 * N_OUT - 2)])
            pe.wait_ge(slab_made, 2 * N_OUT)
            before = 2 * N_OUT * (N_OUT - 1)
            w_free = ((gated_a, 2 * N_OUT), (gated_b, 2 * N_OUT), (x_added, before + 2), (x_added, before + 4))
            for t in range(WOUT_LEN):
                slab_chunk(WOUT_AT, t, t, t // 2 % 2, [w_free[t // 2]])
            turn_normed(1, [(slab_made, 2 * N_OUT), (slab_made, 2 * N_OUT), (prob_t_made, N_HEADS), (u_made, N_HEADS)])

            added0 = 2 * N_OUT * N_OUT
            for t in range(FFN0_LEN):
                column_chunk(FFN0_AT, t, t % 8, t // 8, [(x_added, added0)], h_from=KT if t < 8 else None)
            with pe.Fori(1, N_SLAB) as i:
                at = (FFN_AT - FFN_LEN) + FFN_LEN * i
                added = (added0 - 2 * N_OUT) + 2 * N_OUT * i
                w_free = ((swiglu_made, 2 * i), (silu_made, 2 * i + 2), (x_added, added + 2), (x_added, added + 4))
                for t in range(FFN_LEN):
                    if t < 8:
                        column_chunk(at, t, t, 0, [(x_added, added), (silu_made, 2 * i)])
                    elif t < 16:
                        if t == 8:
                            pe.wait_ge(slab_made, 2 * N_OUT + 2 * i)
                        slab_chunk(at, t, t - 8, (t - 6) // 2 % 2, [w_free[(t - 8) // 2]])
                    else:
                        column_chunk(at, t, t - 16, 1, [(x_added, added + 6)])
                    if t == 2:
                        turn((swiglu_made, 2 * i), [(slab_made, 2 * (N_OUT - 1) + 2 * i), (h_made, 2 * KT)])
            turn((swiglu_made, 2 * N_SLAB), [(slab_made, 2 * (N_OUT + N_SLAB - 1))])
            pe.wait_ge(slab_made, 2 * (N_OUT + N_SLAB))
            before = 2 * N_OUT * (N_OUT + N_SLAB - 1)
            w_free = ((x_added, before), (swiglu_made, 2 * N_SLAB), (x_added, before + 2), (x_added, before + 4))
            for t in range(TAIL_LEN):
                slab_chunk(TAIL_AT, t, t, t // 2 % 2, [w_free[t // 2]])


def bucket_rows():
    dist = SEQ - 1 - np.arange(SKEW)
    far = np.maximum(dist, 1).astype(np.float32) / np.float32(BUCKETS // 2)
    large = BUCKETS // 2 + (np.log(far) / np.float32(np.log(2048 / (BUCKETS // 2)))
                            * np.float32(BUCKETS // 2)).astype(np.int32)
    bucket = np.where(dist < BUCKETS // 2, np.maximum(dist, 0), np.minimum(large, BUCKETS - 1))
    rows = np.zeros((BUCKETS + 1, 4, SKEW), np.float32)
    for g, (window, dilation) in enumerate(((128, 1), (512, 4), (2048, 16), (SEQ, 1))):
        seen = (dist >= 0) & (dist <= window) & (dist % dilation == 0)
        rows[np.where(seen, bucket, BUCKETS), g, np.arange(SKEW)] = 1.0
    return rows


_INS = ("x", "w_in", "w_out_a", "w_out_b", "w_out", "w_ff_gate", "w_ff_up", "w_ff_down", "g_mix", "g_ffn",
        "g_final", "rel_bias")


def kernel(**inputs):
    import concourse.bacc as bacc
    from concourse.bass_utils import run_bass_kernel_spmd

    nc = bacc.Bacc("TRN2", target_bir_lowering=False, num_devices=1)
    f32 = mybir.dt.float32
    arrays = {f"in_{name}": np.ascontiguousarray(inputs[name]) for name in _INS}
    arrays["in_onehot"] = bucket_rows()
    args = [nc.dram_tensor(name, a.shape, f32, kind="ExternalInput").ap() for name, a in arrays.items()]
    out = nc.dram_tensor("out", (1, SEQ, D), f32, kind="ExternalOutput").ap()
    bias_rows = nc.dram_tensor("bias_rows", (N_HEADS, P * (SKEW + 1)), f32, kind="Internal").ap()
    build(nc, *args, out, bias_rows)
    r = run_bass_kernel_spmd(nc, [arrays], core_ids=[0])
    return r.results[0]["out"]
```

```python
import concourse.bass as bass
from concourse import mybir
from contextlib import ExitStack
import numpy as np

P = 128
SEQ = 256
BLK = SEQ // P
D = 2048
KT = D // P
HD = 128
N_GROUP_A, QUAD = 3, 4
N_QUAD_B = 2
N_QUAD = N_GROUP_A + N_QUAD_B
QW = QUAD * HD
WIDTH_A = N_GROUP_A * QW
WIDTH_B = N_QUAD_B * QW
N_IDX, IDX = 16, 64
D_FF = 5632
BUCKETS = 32
N_HEADS = N_QUAD * QUAD
TOPK = 64
EPS = 1e-6
NEG = -1e30
TAKEN = -3e38
COL_Q_A, COL_K_A, COL_V_A = 0, WIDTH_A, 2 * WIDTH_A
COL_Q_B = 3 * WIDTH_A
COL_K_B, COL_V_B = COL_Q_B + WIDTH_B, COL_Q_B + 2 * WIDTH_B
COL_QI = COL_Q_B + 3 * WIDTH_B
COL_KI = COL_QI + N_IDX * IDX
KIW = IDX + N_IDX
COL_GA = COL_KI + KIW
COL_GB = COL_GA + D
NC_ = 512
N_OUT = D // NC_
N_SLAB = D_FF // NC_
SKEW = 3 * P
RING = 4
AHEAD = RING - 1

IDX_AT, IDX_LEN = 0, 24
QUAD_AT, QUAD_LEN = 24, 24
MERGE0_AT = QUAD_AT + N_QUAD * QUAD_LEN
MERGE_AT, MERGE_LEN = MERGE0_AT + 24, 32
MERGE3_AT, MERGE3_LEN = MERGE_AT + (N_OUT - 2) * MERGE_LEN, 24
WOUT_AT, WOUT_LEN = MERGE3_AT + MERGE3_LEN, 16
FFN0_AT, FFN0_LEN = WOUT_AT + WOUT_LEN, 16
FFN_AT, FFN_LEN = FFN0_AT + FFN0_LEN, 24
FFN10_AT = FFN_AT + (N_SLAB - 2) * FFN_LEN
DOWN_AT, DOWN_LEN = FFN10_AT + FFN0_LEN, 16
YA_KTS = (2, 1, 1)
YB_KTS = (2, 2, 2, 1, 1)
MERGE3_KTS = (2,) * 16 + YA_KTS + YB_KTS
MERGE_KTS = (2,) * 24 + YA_KTS + YB_KTS


def build(nc, x, w_in, w_out_a, w_out_b, w_out, w_gate, w_up, w_down, g_mix, g_ffn, g_final,
          rel_bias, onehot, out, bias_rows):
    f32, f32r = mybir.dt.float32, mybir.dt.float32r
    ACT, ALU, AX = mybir.ActivationFunctionType, mybir.AluOpType, mybir.AxisListType
    w_in, w_out_a, w_out_b, w_out = w_in[0], w_out_a[0], w_out_b[0], w_out[0]
    w_gate, w_up, w_down = w_gate[0], w_up[0], w_down[0]

    ctx = ExitStack()
    with ctx:
        def sb(name, shape, dt=f32):
            return ctx.enter_context(nc.sbuf_tensor(name, shape, dt))

        def sem(name):
            return ctx.enter_context(nc.semaphore(name))

        xs = sb("xs", [P, BLK, D])
        h_hi = sb("h_hi", [P, KT, SEQ], f32r)
        h_lo = sb("h_lo", [P, KT, SEQ], f32r)
        raw = sb("raw", [P, RING, 2, NC_])
        w_hi = sb("w_hi", [P, RING, 2, NC_], f32r)
        w_lo = sb("w_lo", [P, RING, 2, NC_], f32r)
        bias = sb("bias", [P, N_HEADS, SKEW])
        u = sb("u", [P, N_QUAD, BLK, QW])
        y_hi = sb("y_hi", [P, 3 * QUAD, SEQ], f32r)
        y_lo = sb("y_lo", [P, 3 * QUAD, SEQ], f32r)
        slab_hi = sb("slab_hi", [P, QUAD, SEQ], f32r)
        slab_lo = sb("slab_lo", [P, QUAD, SEQ], f32r)
        stage = sb("stage", [P, BLK, QW])
        qk = sb("qk", [P, 2, QUAD, SEQ])
        v = sb("v", [P, BLK, QW])
        att = sb("att", [P, 6, SKEW])
        score = [att[:, j, :] for j in range(2)]
        prob = [att[:, 2 + j, :] for j in range(2)]
        prob_t = [att[:, 4 + j, :] for j in range(2)]
        ident = sb("ident", [P, P])
        g_rows = sb("g_rows", [2 * KT, P])
        g_cols = sb("g_cols", [P, 2 * KT])
        rel = sb("rel", [BUCKETS + 1, N_HEADS])
        neg_max = sb("neg_max", [P, N_QUAD, BLK * QUAD])
        denom = sb("denom", [P, N_QUAD, BLK * QUAD])
        mix = sb("mix", [P, 8, BLK * QUAD])
        sq = sb("sq", [P, 3, BLK, N_OUT])
        norm = sb("norm", [P, 3, 7, BLK])
        inv_rms = norm[:, :, 6, :]
        top = sb("top", [P, BLK, 8])
        w_idx = sb("w_idx", [P, BLK, N_IDX])
        flat_u = u[:].rearrange("p a b n -> p (a b n)")
        xg = flat_u[:, 0:BLK * D].rearrange("p (b n) -> p b n", b=BLK)
        qi_t = flat_u[:, 0:2048].rearrange("p (t s) -> p t s", t=8)
        ki_t = flat_u[:, 2048:2304]
        ki_twice = flat_u[:, 2304:2560].rearrange("p (b n) -> p b n", b=BLK)
        relu = [flat_u[:, 2560 + SKEW * j:2560 + SKEW * (j + 1)] for j in range(2)]
        idx_score = flat_u[:, BLK * D:BLK * D + SKEW]
        idx_left = flat_u[:, BLK * D + SKEW:BLK * D + 2 * SKEW]
        hot = qk[0:BUCKETS + 1].rearrange("p a j s -> p (a j s)")[:, 0:4 * SKEW] \
            .rearrange("p (g m) -> p g m", g=4)
        rows_sb = att[0:8, 0:4, :]
        sig_a, sig_b = [qk[:, i, :, :].rearrange("p j s -> p (j s)")
                        .rearrange("p (b n) -> p b n", b=BLK) for i in range(2)]
        silu = sig_a
        spare = v
        g_last = bias[:].rearrange("p h m -> p (h m)")[:, 0:D]

        acc = [[ctx.enter_context(nc.psum_tensor(f"acc{s}{b}", [P, NC_], f32)) for b in range(BLK)]
               for s in range(2)]
        tp = [ctx.enter_context(nc.psum_tensor(f"tp{b}", [P, NC_], f32)) for b in range(2)]
        pt = ctx.enter_context(nc.psum_tensor("pt", [P, NC_], f32))
        po = ctx.enter_context(nc.psum_tensor("po", [P, NC_], f32))
        four = [tp[0], tp[1], pt, po]
        dots = [pt, po]

        x_loaded = [sem(f"x_loaded{q}") for q in range(N_OUT)]
        g_loaded, hot_loaded, rel_loaded, g_last_loaded = sem("g_loaded"), sem("hot_loaded"), sem("rel_loaded"), sem("g_last_loaded")
        ident_zero, ident_made, rel_masked, idx_zero = sem("ident_zero"), sem("ident_made"), sem("rel_masked"), sem("idx_zero")
        bias_rows_made, bias_rows_out, bias_rows_stored, bias_loaded, bias_chosen, bias_step = sem("bias_rows_made"), sem("bias_rows_out"), sem("bias_rows_stored"), sem("bias_loaded"), sem("bias_chosen"), sem("bias_step")
        g_turned, g_out = sem("g_turned"), sem("g_out")
        squares, mean_made, root_made, scale_made, norm_step = sem("squares"), sem("mean_made"), sem("root_made"), sem("scale_made"), sem("norm_step")
        h_turned, h_hi_made, h_made = sem("h_turned"), sem("h_hi_made"), sem("h_made")
        raw_loaded = [sem(f"raw_loaded{s}") for s in range(RING)]
        hi_made, lo_made, chunk_used = sem("hi_made"), sem("lo_made"), sem("chunk_used")
        stage_made, stage_turned = sem("stage_made"), sem("stage_turned")
        ki_made, w_idx_made, ki_turned, ki_t_made, qi_t_made = sem("ki_made"), sem("w_idx_made"), sem("ki_turned"), sem("ki_t_made"), sem("qi_t_made")
        dots_made, relu_made, idx_added, top_step = sem("dots_made"), sem("relu_made"), sem("idx_added"), sem("top_step")
        qk_made, v_made = sem("qk_made"), sem("v_made")
        scored, biased, max_made, exp_made = sem("scored"), sem("biased"), sem("max_made"), sem("exp_made")
        prob_turned, prob_t_made, pv_made, u_made = sem("prob_turned"), sem("prob_t_made"), sem("pv_made"), sem("u_made")
        mix_step, mix_in, mix_exp = sem("mix_step"), sem("mix_in"), sem("mix_exp")
        part_hi, y_made, slab_made = sem("part_hi"), sem("y_made"), sem("slab_made")
        sig_made, gated_a, gated_b, merged = sem("sig_made"), sem("gated_a"), sem("gated_b"), sem("merged")
        silu_made, swiglu_made, x_added = sem("silu_made"), sem("swiglu_made"), sem("x_added")
        xg_made, out_made, out_stored = sem("xg_made"), [sem("out_made_act"), sem("out_made_dve")], sem("out_stored")

        FILL_QI = (0, 1)
        FILL_Q0, FILL_K0 = 2, 3
        FILL_Y = 2 + 2 * N_QUAD
        FILL_SLAB = FILL_Y + 3

        block = ctx.enter_context(nc.Block())

        @block.sync
        def _(sp):
            def load(at, t, src, turn=0):
                slot, c = t % RING, at + t
                if not (isinstance(at, int) and c < RING):
                    sp.wait_ge(lo_made, c - RING + 1)
                kts, width = src.shape[0] // P, src.shape[1]
                sp.dma_start(raw[:, slot, 0:kts, 0:width], src.rearrange("(t p) n -> p t n", p=P)) \
                    .then_inc(raw_loaded[slot], 16)

            def column(at, t0, w, col, width=NC_):
                for k in range(KT // 2):
                    load(at, t0 + k, w[2 * k * P:2 * (k + 1) * P, bass.ds(col, width)])

            def row_slab(at, t0, w, row):
                for n in range(N_OUT):
                    for k in range(2):
                        load(at, t0 + 2 * n + k, w[bass.ds(row + 2 * k * P, 2 * P), n * NC_:(n + 1) * NC_])

            def outs(at, t0, col):
                t = t0
                for w, kts in ((w_out_a, YA_KTS), (w_out_b, YB_KTS)):
                    row = 0
                    for k in kts:
                        load(at, t, w[row:row + k * P, bass.ds(col, NC_)])
                        row, t = row + k * P, t + 1

            column(IDX_AT, 0, w_in, COL_QI)
            column(IDX_AT, 8, w_in, COL_KI, KIW)
            column(IDX_AT, 16, w_in, COL_QI + NC_)
            with sp.Fori(0, N_GROUP_A) as i:
                for n, col in enumerate((COL_Q_A, COL_K_A, COL_V_A)):
                    column(QUAD_AT + QUAD_LEN * i, 8 * n, w_in, col + QW * i)
            with sp.Fori(0, N_QUAD_B) as i:
                for n, col in enumerate((COL_Q_B, COL_K_B, COL_V_B)):
                    column(QUAD_AT + N_GROUP_A * QUAD_LEN + QUAD_LEN * i, 8 * n, w_in, col + QW * i)
            column(MERGE0_AT, 0, w_in, COL_GA)
            column(MERGE0_AT, 8, w_in, COL_GB)
            outs(MERGE0_AT, 16, 0)
            with sp.Fori(0, N_OUT - 2) as n:
                at = MERGE_AT + MERGE_LEN * n
                column(at, 0, w_in, COL_GA + NC_ + NC_ * n)
                row_slab(at, 8, w_out, NC_ * n)
                column(at, 16, w_in, COL_GB + NC_ + NC_ * n)
                outs(at, 24, NC_ + NC_ * n)
            column(MERGE3_AT, 0, w_in, COL_GA + (N_OUT - 1) * NC_)
            column(MERGE3_AT, 8, w_in, COL_GB + (N_OUT - 1) * NC_)
            outs(MERGE3_AT, 16, (N_OUT - 1) * NC_)
            for s in range(2):
                row_slab(WOUT_AT, 8 * s, w_out, (N_OUT - 2 + s) * NC_)
            column(FFN0_AT, 0, w_gate, 0)
            column(FFN0_AT, 8, w_up, 0)
            with sp.Fori(1, N_SLAB - 1) as i:
                at = (FFN_AT - FFN_LEN) + FFN_LEN * i
                column(at, 0, w_gate, NC_ * i)
                row_slab(at, 8, w_down, NC_ * i - NC_)
                column(at, 16, w_up, NC_ * i)
            column(FFN10_AT, 0, w_gate, (N_SLAB - 1) * NC_)
            column(FFN10_AT, 8, w_up, (N_SLAB - 1) * NC_)
            for s in range(2):
                row_slab(DOWN_AT, 8 * s, w_down, (N_SLAB - 2 + s) * NC_)
            for n in range(2 * BLK):
                sp.wait_ge(*((out_made[1], n + 1) if n < 3 else (out_made[0], 1)))
                rows, cols = slice(n // 2 * P, (n // 2 + 1) * P), slice(n % 2 * D // 2, (n % 2 + 1) * D // 2)
                sp.dma_start(out[0, rows, cols], xg[:, n // 2, cols]).then_inc(out_stored, 16)
            sp.wait_ge(out_stored, 16 * 2 * BLK)

        @block.gpsimd
        def _(pool):
            pool.dma_start(hot, onehot).then_inc(hot_loaded, 16)
            pool.dma_start(rel[0:BUCKETS, :], rel_bias).then_inc(rel_loaded, 16)
            pool.memset(rel[BUCKETS:BUCKETS + 1, :], NEG).then_inc(rel_masked, 1)
            pool.wait_ge(rel_masked, 1)
            pool.memset(ident[:], 0.0).then_inc(ident_zero, 1)
            pool.wait_ge(ident_zero, 1)
            pool.affine_select(out=ident[:], in_=ident[:], compare_op=ALU.not_equal, fill=1.0, base=0,
                               pattern=[[-1, P]], channel_multiplier=1).then_inc(ident_made, 1)
            pool.memset(idx_score, 0.0).then_inc(idx_zero, 1)
            pool.wait_ge(idx_zero, 1)
            pool.affine_select(out=idx_score[:, 0:P], in_=idx_score[:, 0:P], compare_op=ALU.is_ge, fill=NEG,
                               base=0, pattern=[[-1, P]], channel_multiplier=1).then_inc(idx_zero, 1)
            pool.affine_select(out=idx_score[:, P:SKEW], in_=idx_score[:, P:SKEW], compare_op=ALU.is_ge,
                               fill=NEG, base=P, pattern=[[-1, SEQ]], channel_multiplier=1).then_inc(idx_zero, 1)
            for g in range(4):
                n = 4 if g < 3 else 8
                pool.wait_ge(bias_rows_out, g + 1)
                pool.dma_start(bias_rows[4 * g:4 * g + n].rearrange("h (q m) -> h q m", q=P)[:, :, 0:SKEW],
                               rows_sb[0:n, g, :].unsqueeze(1).to_broadcast([n, P, SKEW])) \
                    .then_inc(bias_rows_stored, 16)
            pool.wait_ge(bias_rows_stored, 4 * 16)
            for a in range(N_QUAD):
                skewed = bias_rows[4 * a:4 * a + QUAD, 0:P * SKEW].rearrange("h (q m) -> q h m", q=P)
                for lo, width, at in ((P, P, 0), (0, SEQ, P)):
                    src = bass.AP(skewed.tensor, skewed.offset + P - 1 + lo, [*skewed.ap[:2], [1, width]])
                    pool.dma_start(bias[:, 4 * a:4 * a + QUAD, at:at + width], src).then_inc(bias_loaded, 16)
            pool.wait_ge(bias_loaded, 2 * N_QUAD * 16)
            pool.wait_ge(top_step, 4 * TOPK // 8)
            pool.tensor_scalar(idx_left, idx_left, TAKEN / 2, NEG, ALU.is_gt, ALU.mult).then_inc(bias_step, 1)
            pool.wait_ge(bias_step, 1)
            for h in range(N_GROUP_A * QUAD, N_HEADS):
                pool.tensor_tensor(bias[:, h, :], bias[:, h, :], idx_left, ALU.add).then_inc(bias_chosen, 1)
            pool.wait_ge(biased, N_HEADS)
            pool.dma_start(g_last, g_final.partition_broadcast(P)).then_inc(g_last_loaded, 16)

        @block.scalar
        def _(act):
            def hi(at, t, turn, kts=2, width=NC_):
                slot = t % RING
                act.wait_ge(raw_loaded[slot], 16 * (turn + t // RING + 1))
                if not (isinstance(at, int) and at + t < RING):
                    act.wait_ge(chunk_used, at + t - RING + 1)
                act.activation(w_hi[:, slot, 0:kts, 0:width], raw[:, slot, 0:kts, 0:width], ACT.Copy) \
                    .then_inc(hi_made, 1)

            def copy_stage(last_chunk, s, fill):
                act.wait_ge(chunk_used, last_chunk + 1)
                act.wait_ge(stage_turned, fill)
                act.activation(stage[:, 0, :], acc[s][0][:], ACT.Copy, scale=inv_rms[:, 0, 0:1]).then_inc(stage_made, 1)

            def copy_turned(dst, fill, done):
                act.wait_ge(stage_turned, fill + 1)
                act.activation(dst[:, :, 0:P], tp[0][:].rearrange("p (j s) -> p j s", j=QUAD), ACT.Copy) \
                    .then_inc(done, 1)

            def hi_turned(dst, fill):
                act.wait_ge(stage_turned, fill + 1)
                for b in range(BLK):
                    act.activation(dst[:, :, b * P:(b + 1) * P], tp[b][:].rearrange("p (j s) -> p j s", j=QUAD),
                                   ACT.Copy).then_inc(part_hi, 1)

            def exps(a, j):
                act.wait_ge(max_made, 8 * a + 2 * j + 2)
                if j >= 2:
                    act.wait_ge(prob_turned, 4 * a + j - 1)
                for b, cols in ((0, slice(0, P)), (1, slice(P, SKEW))):
                    i = b * QUAD + j
                    act.activation(prob[j % 2][:, cols], score[j % 2][:, cols], ACT.Exp,
                                   bias=neg_max[:, a, i:i + 1], accum_out=denom[:, a, i:i + 1]) \
                        .then_inc(exp_made, 1)

            def copy_prob(a, j):
                act.wait_ge(prob_turned, 4 * a + j + 1)
                if j >= 2:
                    act.wait_ge(pv_made, 4 * a + j - 1)
                act.activation(prob_t[j % 2], pt[:, 0:SKEW], ACT.Copy).then_inc(prob_t_made, 1)

            def attend(a, t):
                if t in (-1, 0, 2, 4):
                    exps(a, (-1, 0, 2, 4).index(t))
                if t in (1, 3, 5, 7):
                    copy_prob(a, (1, 3, 5, 7).index(t))

            def quad(at, i, t):
                if t == 7:
                    copy_stage(at + 7, 1, FILL_Q0 + 2 * i)
                if t == 10:
                    copy_turned(qk[:, 0], FILL_Q0 + 2 * i, qk_made)
                if t == 15:
                    copy_stage(at + 15, 0, FILL_K0 + 2 * i)
                if t == 18:
                    copy_turned(qk[:, 1], FILL_K0 + 2 * i, qk_made)
                if t == 23:
                    act.wait_ge(chunk_used, at + 24)
                    act.activation(v[:, 0, :], acc[1][0][:], ACT.Copy, scale=inv_rms[:, 0, 0:1]).then_inc(v_made, 1)

            def gates(at, t, s, dst, before):
                act.wait_ge(chunk_used, at + t + 1)
                if before is not None:
                    act.wait_ge(*before)
                for b in range(BLK):
                    act.activation(dst[:, b, :], acc[s][b][:], ACT.Sigmoid, scale=inv_rms[:, 0, b:b + 1]) \
                        .then_inc(sig_made, 1)

            def square_part(which, n):
                if which + n:
                    act.wait_ge(squares, 2 * N_OUT * which + 2 * n)
                for b in range(BLK):
                    act.activation(spare[:, b, :], xs[:, b, n * NC_:(n + 1) * NC_], ACT.Square,
                                   accum_out=sq[:, which, b, n:n + 1]).then_inc(squares, 1)

            def root(which):
                act.wait_ge(mean_made, which + 1)
                act.activation(norm[:, which, 1, :], norm[:, which, 0, :], ACT.Sqrt).then_inc(root_made, 1)

            def hi_rows(which, q):
                for k in range(4 * q, 4 * q + 4):
                    act.wait_ge(h_turned, KT * which + k // 2 * 2 + 2)
                    act.activation(h_hi[:, k, :], four[k // 2 % 4][:, k % 2 * SEQ:(k % 2 + 1) * SEQ], ACT.Copy,
                                   scale=g_cols[:, KT * which + k:KT * which + k + 1]).then_inc(h_hi_made, 1)

            act.dma_start(g_rows[0:KT, :], g_mix.rearrange("a (k p) -> (a k) p", p=P)).then_inc(g_loaded, 16)
            act.dma_start(g_rows[KT:2 * KT, :], g_ffn.rearrange("a (k p) -> (a k) p", p=P)).then_inc(g_loaded, 16)
            for q in range(N_OUT):
                cols = slice(q * NC_, (q + 1) * NC_)
                act.dma_start(xs[:, :, cols], x[0, :, cols].rearrange("(b p) n -> p b n", p=P)) \
                    .then_inc(x_loaded[q], 16)
            hi(IDX_AT, 0, 0)
            act.wait_ge(g_out, 1)
            hi_rows(0, 0)
            hi(IDX_AT, 1, 0)
            hi(IDX_AT, 2, 0)

            for t in range(IDX_LEN):
                hi(IDX_AT, t + AHEAD, 0, width=KIW if 8 <= t + AHEAD < 16 else NC_)
                if t in (0, 2, 4):
                    hi_rows(0, 1 + t // 2)
                if t < 4:
                    act.wait_ge(x_loaded[t], 16)
                    square_part(0, t)
                if t == 5:
                    root(0)
                if t == 7:
                    act.wait_ge(scale_made, 1)
                    copy_stage(IDX_AT + 7, 0, FILL_QI[0])
                if t == 9:
                    copy_turned(qi_t[:, 0:4], FILL_QI[0], qi_t_made)
                if t == 17:
                    act.wait_ge(ki_turned, 1)
                    act.activation(ki_t[:, 0:P], tp[0][:, 0:P], ACT.Copy).then_inc(ki_t_made, 1)
                if t == 23:
                    copy_stage(IDX_AT + 23, 0, FILL_QI[1])

            for t in range(QUAD_LEN):
                hi(QUAD_AT, t + AHEAD, QUAD_AT // RING)
                if t == 1:
                    copy_turned(qi_t[:, 4:8], FILL_QI[1], qi_t_made)
                if 2 <= t < 2 + N_IDX:
                    h = t - 2
                    act.wait_ge(dots_made, h + 1)
                    if h >= 2:
                        act.wait_ge(idx_added, 2 * (h - 1))
                    act.activation(relu[h % 2], dots[h % 2][:, 0:SKEW], ACT.Relu).then_inc(relu_made, 1)
                quad(QUAD_AT, 0, t)

            with act.Fori(1, N_QUAD) as i:
                at = QUAD_AT + QUAD_LEN * i
                attend(i - 1, -1)
                for t in range(QUAD_LEN):
                    hi(at, t + AHEAD, QUAD_AT // RING + QUAD_LEN // RING * i)
                    attend(i - 1, t)
                    quad(at, i, t)

            attend(N_QUAD - 1, -1)
            for t in range(MERGE3_LEN):
                nxt = t + AHEAD
                hi(MERGE0_AT, nxt, MERGE0_AT // RING, MERGE3_KTS[nxt] if nxt < MERGE3_LEN else 2)
                attend(N_QUAD - 1, t)
                if t == 8:
                    act.wait_ge(mix_in, 1)
                    act.activation(mix[:, 4:7, :], mix[:, 1:4, :], ACT.Exp).then_inc(mix_exp, 1)
                if t == 9:
                    gates(MERGE0_AT, 7, 0, sig_a, (scored, N_HEADS))
                if t in (12, 14, 16):
                    n = (t - 12) // 2
                    hi_turned(y_hi[:, QUAD * n:QUAD * (n + 1)], FILL_Y + n)
                if t == 15:
                    gates(MERGE0_AT, 15, 1, sig_b, None)
            with act.Fori(1, N_OUT - 1) as n:
                at = (MERGE_AT - MERGE_LEN) + MERGE_LEN * n
                turn = (MERGE_AT - MERGE_LEN) // RING + MERGE_LEN // RING * n
                for t in range(MERGE_LEN):
                    nxt = t + AHEAD
                    hi(at, nxt, turn, MERGE_KTS[nxt] if nxt < MERGE_LEN else 2)
                    if t == 2:
                        hi_turned(slab_hi[:], FILL_SLAB - 1 + n)
                    if t == 7:
                        gates(at, 7, 0, sig_a, (gated_a, 2 * n))
                    if t == 23:
                        gates(at, 23, 1, sig_b, (merged, n))
            for t in range(MERGE3_LEN):
                nxt = t + AHEAD
                hi(MERGE3_AT, nxt, MERGE3_AT // RING, MERGE3_KTS[nxt] if nxt < MERGE3_LEN else 2)
                if t == 2:
                    hi_turned(slab_hi[:], FILL_SLAB + N_OUT - 2)
                if t == 7:
                    gates(MERGE3_AT, 7, 0, sig_a, (gated_a, 2 * (N_OUT - 1)))
                if t == 15:
                    gates(MERGE3_AT, 15, 1, sig_b, (merged, N_OUT - 1))
            for t in range(WOUT_LEN):
                hi(WOUT_AT, t + AHEAD, WOUT_AT // RING)
                if t == 2:
                    hi_turned(y_hi[:, 0:QUAD], FILL_SLAB + N_OUT - 1)
                if t in (9, 11, 13, 15):
                    act.wait_ge(x_added, 2 * N_OUT * (N_OUT - 1) + t - 7)
                    square_part(1, (t - 9) // 2)
                if t in (11, 13, 15):
                    hi_rows(1, (t - 11) // 2)

            def silu_gate(at, i):
                act.wait_ge(chunk_used, at + 8)
                for b in range(BLK):
                    act.activation(silu[:, b, :], acc[0][b][:], ACT.Silu, scale=inv_rms[:, 1, b:b + 1]) \
                        .then_inc(silu_made, 1)

            for t in range(FFN0_LEN):
                hi(FFN0_AT, t + AHEAD, FFN0_AT // RING)
                if t == 1:
                    hi_rows(1, 3)
                if t == 2:
                    root(1)
                if t == 7:
                    act.wait_ge(scale_made, 2)
                    silu_gate(FFN0_AT, 0)
            with act.Fori(1, N_SLAB - 1) as i:
                at = (FFN_AT - FFN_LEN) + FFN_LEN * i
                for t in range(FFN_LEN):
                    hi(at, t + AHEAD, (FFN_AT - FFN_LEN) // RING + FFN_LEN // RING * i)
                    if t == 2:
                        hi_turned(slab_hi[:], FILL_SLAB + N_OUT - 1 + i)
                    if t == 7:
                        silu_gate(at, i)
            for t in range(FFN0_LEN):
                hi(FFN10_AT, t + AHEAD, FFN10_AT // RING)
                if t == 2:
                    hi_turned(slab_hi[:], FILL_SLAB + N_OUT + N_SLAB - 2)
                if t == 7:
                    silu_gate(FFN10_AT, N_SLAB - 1)
            for t in range(DOWN_LEN):
                if t + AHEAD < DOWN_LEN:
                    hi(DOWN_AT, t + AHEAD, DOWN_AT // RING)
                if t == 2:
                    hi_turned(y_hi[:, 0:QUAD], FILL_SLAB + N_OUT + N_SLAB - 1)
                if t == 4:
                    act.activation(norm[:, 2, 1, :], norm[:, 1, 0, :], ACT.Sqrt)
                if t in (9, 11, 13, 15):
                    act.wait_ge(x_added, 2 * N_OUT * (N_OUT + N_SLAB - 1) + t - 7)
                    square_part(2, (t - 9) // 2)
            root(2)
            act.wait_ge(scale_made, 3)
            act.wait_ge(xg_made, 2 * N_OUT)
            act.activation(xg[:, 1, D // 2:D], xg[:, 1, D // 2:D], ACT.Copy, scale=inv_rms[:, 2, 1:2]) \
                .then_inc(out_made[0], 1)

        @block.vector
        def _(dve):
            class Chain:

                def __init__(self, s):
                    self.s, self.n = s, 0

                def then(self, ins):
                    self.n += 1
                    ins.then_inc(self.s, 1)
                    dve.wait_ge(self.s, self.n)

            def lo(at, t, kts=2, width=NC_):
                slot = t % RING
                dve.wait_ge(hi_made, at + t + 1)
                dve.tensor_tensor(w_lo[:, slot, 0:kts, 0:width], raw[:, slot, 0:kts, 0:width],
                                  w_hi[:, slot, 0:kts, 0:width].bitcast(f32), ALU.subtract).then_inc(lo_made, 1)

            def copy_stage(last_chunk, s, fill):
                dve.wait_ge(chunk_used, last_chunk + 1)
                dve.wait_ge(stage_turned, fill)
                dve.tensor_scalar(stage[:, 1, :], acc[s][1][:], inv_rms[:, 0, 1:2], None, ALU.mult).then_inc(stage_made, 1)

            def copy_turned(dst, fill, done):
                dve.wait_ge(stage_turned, fill + 1)
                dve.tensor_copy(dst[:, :, P:SEQ], tp[1][:].rearrange("p (j s) -> p j s", j=QUAD)).then_inc(done, 1)

            def lo_turned(dst, of, fill, done):
                for b in range(BLK):
                    dve.wait_ge(part_hi, 2 * (fill - FILL_Y) + b + 1)
                    cols = slice(b * P, (b + 1) * P)
                    dve.tensor_tensor(dst[:, :, cols], tp[b][:].rearrange("p (j s) -> p j s", j=QUAD),
                                      of[:, :, cols].bitcast(f32), ALU.subtract).then_inc(done, 1)

            def scores(a, j):
                dve.wait_ge(scored, 4 * a + j + 1)
                if j >= 2:
                    dve.wait_ge(exp_made, 8 * a + 2 * (j - 1))
                dve.scalar_tensor_tensor(out=score[j % 2], in0=tp[j % 2][:, 0:SKEW], scalar=HD ** -0.5,
                                         in1=bias[:, 4 * a + j, :], op0=ALU.mult, op1=ALU.add).then_inc(biased, 1)
                dve.wait_ge(biased, 4 * a + j + 1)
                for b, cols in ((0, slice(0, P)), (1, slice(P, SKEW))):
                    i = b * QUAD + j
                    dve.tensor_reduce(neg_max[:, a, i:i + 1], score[j % 2][:, cols], AX.X, ALU.max,
                                      negate=True).then_inc(max_made, 1)

            def copy_out(a, j):
                dve.wait_ge(pv_made, 4 * a + j + 1)
                dve.tensor_copy(u[:, a, :, j * HD:(j + 1) * HD],
                                po[:, 0:SEQ].rearrange("p (b d) -> p b d", b=BLK)).then_inc(u_made, 1)

            def attend(a, t):
                if t == -1:
                    scores(a, 0)
                    scores(a, 1)
                if t in (2, 4):
                    scores(a, 2 + (t - 2) // 2)
                if t in (3, 5, 7, 9):
                    copy_out(a, (t - 3) // 2)

            def quad(at, i, t):
                if t == 7:
                    copy_stage(at + 7, 1, FILL_Q0 + 2 * i)
                if t == 10:
                    copy_turned(qk[:, 0], FILL_Q0 + 2 * i, qk_made)
                if t == 15:
                    copy_stage(at + 15, 0, FILL_K0 + 2 * i)
                if t == 18:
                    copy_turned(qk[:, 1], FILL_K0 + 2 * i, qk_made)
                if t == 23:
                    dve.wait_ge(chunk_used, at + 24)
                    dve.tensor_scalar(v[:, 1, :], acc[1][1][:], inv_rms[:, 0, 1:2], None, ALU.mult).then_inc(v_made, 1)

            def add_x(at, t, s, n):
                dve.wait_ge(chunk_used, at + t + 1)
                for b in range(BLK):
                    cols = slice(n * NC_, (n + 1) * NC_)
                    dve.tensor_tensor(xs[:, b, cols], acc[s][b][:], xs[:, b, cols], ALU.add).then_inc(x_added, 1)

            def gate_a(at, t, n):
                dve.wait_ge(chunk_used, at + t + 1)
                dve.wait_ge(sig_made, 4 * n + 2)
                dve.wait_ge(stage_turned, FILL_SLAB + n)
                for b in range(BLK):
                    dve.tensor_tensor(stage[:, b, :], acc[0][b][:], sig_a[:, b, :], ALU.mult).then_inc(gated_a, 1)

            def gate_b(at, t, n):
                dve.wait_ge(chunk_used, at + t + 1)
                dve.wait_ge(sig_made, 4 * n + 4)
                for b in range(BLK):
                    dve.tensor_tensor(sig_b[:, b, :], acc[1][b][:], sig_b[:, b, :], ALU.mult).then_inc(gated_b, 1)
                dve.wait_ge(gated_a, 2 * n + 2)
                dve.wait_ge(gated_b, 2 * n + 2)
                dve.tensor_tensor(stage[:], stage[:], sig_b, ALU.add).then_inc(merged, 1)

            norm_chain = Chain(norm_step)

            def mean_rows(which):
                dve.wait_ge(squares, 2 * N_OUT * (which + 1))
                norm_chain.then(dve.tensor_reduce(norm[:, which, 2, :], sq[:, which], AX.X, ALU.add))
                dve.tensor_scalar(norm[:, which, 0, :], norm[:, which, 2, :], 1.0 / D, EPS, ALU.mult, ALU.add) \
                    .then_inc(mean_made, 1)

            def inv_rows(which):
                dve.wait_ge(root_made, which + 1)
                w = norm[:, which]
                norm_chain.then(dve.reciprocal(w[:, 3, :], w[:, 1, :]))
                norm_chain.then(dve.tensor_tensor(w[:, 4, :], w[:, 3, :], w[:, 3, :], ALU.mult))
                norm_chain.then(dve.tensor_tensor(w[:, 5, :], w[:, 4, :], w[:, 0, :], ALU.mult))
                norm_chain.then(dve.tensor_scalar(w[:, 2, :], w[:, 5, :], -0.5, 1.5, ALU.mult, ALU.add))
                dve.tensor_tensor(w[:, 6, :], w[:, 3, :], w[:, 2, :], ALU.mult).then_inc(scale_made, 1)
                dve.wait_ge(scale_made, which + 1)

            def lo_rows(which, q):
                for k in range(4 * q, 4 * q + 4):
                    dve.wait_ge(h_hi_made, KT * which + k // 2 * 2 + 2)
                    dve.scalar_tensor_tensor(out=h_lo[:, k, :], in0=four[k // 2 % 4][:, k % 2 * SEQ:(k % 2 + 1) * SEQ],
                                             scalar=g_cols[:, KT * which + k:KT * which + k + 1],
                                             in1=h_hi[:, k, :].bitcast(f32), op0=ALU.mult,
                                             op1=ALU.subtract).then_inc(h_made, 1)

            def bias_row(g):
                n = 4 if g < 3 else 8
                dve.wait_ge(bias_rows_made, g + 1)
                dve.tensor_copy(rows_sb[0:n, g, :], dots[g % 2][0:n, 0:SKEW]).then_inc(bias_rows_out, 1)

            dve.wait_ge(g_turned, 1)
            dve.tensor_copy(g_cols[:], acc[0][0][:, 0:2 * KT]).then_inc(g_out, 1)
            dve.wait_ge(g_out, 1)
            lo(IDX_AT, 0)
            lo_rows(0, 0)
            lo(IDX_AT, 1)
            lo(IDX_AT, 2)

            for t in range(IDX_LEN):
                lo(IDX_AT, t + AHEAD, width=KIW if 8 <= t + AHEAD < 16 else NC_)
                if t in (0, 2, 4):
                    lo_rows(0, 1 + t // 2)
                if t == 4:
                    mean_rows(0)
                if t == 5:
                    inv_rows(0)
                if t == 7:
                    copy_stage(IDX_AT + 7, 0, FILL_QI[0])
                if t == 9:
                    copy_turned(qi_t[:, 0:4], FILL_QI[0], qi_t_made)
                if t in (10, 11, 18, 19):
                    bias_row((10, 11, 18, 19).index(t))
                if t == 15:
                    dve.wait_ge(chunk_used, IDX_AT + 16)
                    for b in range(BLK):
                        inv = inv_rms[:, 0, b:b + 1]
                        for half in range(2):
                            dve.tensor_scalar(ki_twice[:, b, half * IDX:(half + 1) * IDX], acc[1][b][:, 0:IDX],
                                              inv, None, ALU.mult).then_inc(ki_made, 1)
                        dve.tensor_scalar(w_idx[:, b, :], acc[1][b][:, IDX:KIW], inv,
                                          (IDX ** -0.5) * (N_IDX ** -0.5), ALU.mult, ALU.mult).then_inc(w_idx_made, 1)
                if t == 17:
                    dve.wait_ge(ki_turned, 1)
                    dve.tensor_copy(ki_t[:, P:SEQ], tp[1][:, 0:P]).then_inc(ki_t_made, 1)
                if t == 23:
                    copy_stage(IDX_AT + 23, 0, FILL_QI[1])

            top_chain = Chain(top_step)
            halves = ((0, slice(0, P)), (1, slice(P, SKEW)))

            def top_round(r):
                left = idx_score if r == 0 else idx_left
                for b, cols in halves:
                    ins = dve.max(top[:, b, :], left[:, cols])
                    top_chain.n += 1
                    ins.then_inc(top_step, 1)
                dve.wait_ge(top_step, top_chain.n)
                for b, cols in halves:
                    ins = dve.match_replace(out=idx_left[:, cols], in_to_replace=top[:, b, :],
                                            in_values=left[:, cols], imm_value=TAKEN)
                    top_chain.n += 1
                    ins.then_inc(top_step, 1)
                dve.wait_ge(top_step, top_chain.n)

            for t in range(QUAD_LEN):
                lo(QUAD_AT, t + AHEAD)
                if t == 1:
                    copy_turned(qi_t[:, 4:8], FILL_QI[1], qi_t_made)
                if 2 <= t < 2 + N_IDX:
                    h = t - 2
                    if h == 0:
                        dve.wait_ge(idx_zero, 3)
                    else:
                        dve.wait_ge(idx_added, 2 * h)
                    dve.wait_ge(relu_made, h + 1)
                    for b, cols in halves:
                        dve.scalar_tensor_tensor(out=idx_score[:, cols], in0=relu[h % 2][:, cols],
                                                 scalar=w_idx[:, b, h:h + 1], in1=idx_score[:, cols],
                                                 op0=ALU.mult, op1=ALU.add).then_inc(idx_added, 1)
                quad(QUAD_AT, 0, t)
                if t == 18:
                    dve.wait_ge(idx_added, 2 * N_IDX)
                if t >= 18:
                    top_round(t - 18)
                if t == 22:
                    top_round(6)
            top_round(7)

            def quad_pass(i):
                at = QUAD_AT + QUAD_LEN * i
                attend(i - 1, -1)
                for t in range(QUAD_LEN):
                    lo(at, t + AHEAD)
                    attend(i - 1, t)
                    quad(at, i, t)

            dve.wait_ge(bias_loaded, 2 * N_QUAD * 16)
            with dve.Fori(1, N_GROUP_A + 1) as i:
                quad_pass(i)
            dve.wait_ge(bias_chosen, N_QUAD_B * QUAD)
            quad_pass(N_QUAD - 1)

            mix_chain = Chain(mix_step)

            def spread(weights):
                return weights.unsqueeze(2).to_broadcast([P, BLK * QUAD, HD])

            def heads(rows):
                return rows.rearrange("p b (j d) -> p (b j) d", j=QUAD)

            attend(N_QUAD - 1, -1)
            for t in range(MERGE3_LEN):
                nxt = t + AHEAD
                lo(MERGE0_AT, nxt, MERGE3_KTS[nxt] if nxt < MERGE3_LEN else 2)
                attend(N_QUAD - 1, t)
                if t == 6:
                    dve.wait_ge(u_made, 4 * N_GROUP_A)
                    mix_chain.then(dve.tensor_tensor(mix[:, 0, :], neg_max[:, 0, :], neg_max[:, 1, :], ALU.min))
                    mix_chain.then(dve.tensor_tensor(mix[:, 0, :], mix[:, 0, :], neg_max[:, 2, :], ALU.min))
                    for g in range(N_GROUP_A):
                        ins = dve.tensor_tensor(mix[:, 1 + g, :], mix[:, 0, :], neg_max[:, g, :], ALU.subtract)
                        if g < N_GROUP_A - 1:
                            mix_chain.then(ins)
                    ins.then_inc(mix_in, 1)
                if t == 8:
                    dve.wait_ge(mix_exp, 1)
                    mix_chain.then(dve.tensor_tensor(mix[:, 1:4, :], mix[:, 4:7, :], denom[:, 0:3, :], ALU.mult))
                    mix_chain.then(dve.tensor_tensor(mix[:, 0, :], mix[:, 1, :], mix[:, 2, :], ALU.add))
                    mix_chain.then(dve.tensor_tensor(mix[:, 0, :], mix[:, 0, :], mix[:, 3, :], ALU.add))
                    mix_chain.then(dve.reciprocal(mix[:, 7, :], mix[:, 0, :]))
                    for g in range(N_GROUP_A):
                        mix_chain.then(dve.tensor_tensor(mix[:, 4 + g, :], mix[:, 4 + g, :], mix[:, 7, :], ALU.mult))
                if t in (8, 9, 10):
                    g = t - 8
                    mix_chain.then(dve.tensor_tensor(heads(u[:, g]), heads(u[:, g]), spread(mix[:, 4 + g, :]), ALU.mult))
                if t == 10:
                    mix_chain.then(dve.tensor_tensor(u[:, 0], u[:, 0], u[:, 1], ALU.add))
                if t == 11:
                    dve.wait_ge(stage_turned, FILL_Y)
                    dve.tensor_tensor(stage[:], u[:, 0], u[:, 2], ALU.add).then_inc(stage_made, 2)
                    dve.wait_ge(u_made, N_HEADS)
                    mix_chain.then(dve.reciprocal(mix[:, 0:2, :], denom[:, 3:5, :]))
                if t == 12:
                    lo_turned(y_lo[:, 0:QUAD], y_hi[:, 0:QUAD], FILL_Y, y_made)
                if t in (12, 14):
                    n = (t - 12) // 2
                    dve.wait_ge(stage_turned, FILL_Y + 1 + n)
                    dve.tensor_tensor(heads(stage[:]), heads(u[:, 3 + n]), spread(mix[:, n, :]), ALU.mult) \
                        .then_inc(stage_made, 2)
                if t in (14, 16):
                    n = (t - 12) // 2
                    lo_turned(y_lo[:, QUAD * n:QUAD * (n + 1)], y_hi[:, QUAD * n:QUAD * (n + 1)], FILL_Y + n, y_made)
                if t == 18:
                    gate_a(MERGE0_AT, t, 0)
                if t == 23:
                    gate_b(MERGE0_AT, t, 0)
            with dve.Fori(1, N_OUT - 1) as n:
                at = (MERGE_AT - MERGE_LEN) + MERGE_LEN * n
                for t in range(MERGE_LEN):
                    nxt = t + AHEAD
                    lo(at, nxt, MERGE_KTS[nxt] if nxt < MERGE_LEN else 2)
                    if t == 2:
                        lo_turned(slab_lo[:], slab_hi, FILL_SLAB - 1 + n, slab_made)
                    if t in (9, 11, 13, 15):
                        add_x(at, t, (t - 7) // 2 % 2, (t - 9) // 2)
                    if t == 26:
                        gate_a(at, t, n)
                    if t == 31:
                        gate_b(at, t, n)
            for t in range(MERGE3_LEN):
                nxt = t + AHEAD
                lo(MERGE3_AT, nxt, MERGE3_KTS[nxt] if nxt < MERGE3_LEN else 2)
                if t == 2:
                    lo_turned(slab_lo[:], slab_hi, FILL_SLAB + N_OUT - 2, slab_made)
                if t == 18:
                    gate_a(MERGE3_AT, t, N_OUT - 1)
                if t == 23:
                    gate_b(MERGE3_AT, t, N_OUT - 1)
            for t in range(WOUT_LEN):
                lo(WOUT_AT, t + AHEAD)
                if t == 2:
                    lo_turned(y_lo[:, 0:QUAD], y_hi[:, 0:QUAD], FILL_SLAB + N_OUT - 1, slab_made)
                if t % 2:
                    add_x(WOUT_AT, t, t // 2 % 2, t % 8 // 2)
                if t in (11, 13, 15):
                    lo_rows(1, (t - 11) // 2)

            def swiglu(at, t, i):
                dve.wait_ge(chunk_used, at + t + 1)
                dve.wait_ge(silu_made, 2 * i + 2)
                dve.wait_ge(stage_turned, FILL_SLAB + N_OUT + i)
                for b in range(BLK):
                    dve.scalar_tensor_tensor(out=stage[:, b, :], in0=acc[1][b][:], scalar=inv_rms[:, 1, b:b + 1],
                                             in1=silu[:, b, :], op0=ALU.mult, op1=ALU.mult).then_inc(swiglu_made, 1)

            for t in range(FFN0_LEN):
                lo(FFN0_AT, t + AHEAD)
                if t == 1:
                    lo_rows(1, 3)
                    mean_rows(1)
                if t == 3:
                    inv_rows(1)
                if t == 15:
                    swiglu(FFN0_AT, t, 0)
            with dve.Fori(1, N_SLAB - 1) as i:
                at = (FFN_AT - FFN_LEN) + FFN_LEN * i
                for t in range(FFN_LEN):
                    lo(at, t + AHEAD)
                    if t == 2:
                        lo_turned(slab_lo[:], slab_hi, FILL_SLAB + N_OUT - 1 + i, slab_made)
                    if t in (9, 11, 13, 15):
                        add_x(at, t, (t - 7) // 2 % 2, (t - 9) // 2)
                    if t == 23:
                        swiglu(at, t, i)
            for t in range(FFN0_LEN):
                lo(FFN10_AT, t + AHEAD)
                if t == 2:
                    lo_turned(slab_lo[:], slab_hi, FILL_SLAB + N_OUT + N_SLAB - 2, slab_made)
                if t == 15:
                    swiglu(FFN10_AT, t, N_SLAB - 1)
            dve.wait_ge(g_last_loaded, 16)
            for t in range(DOWN_LEN):
                if t + AHEAD < DOWN_LEN:
                    lo(DOWN_AT, t + AHEAD)
                if t == 2:
                    lo_turned(y_lo[:, 0:QUAD], y_hi[:, 0:QUAD], FILL_SLAB + N_OUT + N_SLAB - 1, slab_made)
                if t % 2:
                    add_x(DOWN_AT, t, t // 2 % 2, t % 8 // 2)
                if t in (9, 11, 13, 15):
                    dve.wait_ge(x_added, 2 * N_OUT * (N_OUT + N_SLAB - 1) + t - 7)
                    cols = slice((t - 9) // 2 * NC_, (t - 7) // 2 * NC_)
                    for b in range(BLK):
                        dve.tensor_tensor(xg[:, b, cols], xs[:, b, cols], g_last[:, cols], ALU.mult) \
                            .then_inc(xg_made, 1)
            mean_rows(2)
            inv_rows(2)
            dve.wait_ge(xg_made, 2 * N_OUT)
            for n in range(3):
                b, cols = n // 2, slice(n % 2 * D // 2, (n % 2 + 1) * D // 2)
                dve.tensor_scalar(xg[:, b, cols], xg[:, b, cols], inv_rms[:, 2, b:b + 1], None, ALU.mult) \
                    .then_inc(out_made[1], 1)

        @block.tensor
        def _(pe):
            def chunk(at, t, x_hi, x_lo, k0, s, first, last, kts=2, width=NC_):
                slot = t % RING
                pe.wait_ge(lo_made, at + t + 1)
                for k in range(kts):
                    for b in range(BLK):
                        rows = slice(b * P, (b + 1) * P)
                        dst = acc[s][b][:, 0:width]
                        a_hi, a_lo = x_hi[:, k0 + k, rows], x_lo[:, k0 + k, rows]
                        b_hi, b_lo = w_hi[:, slot, k, 0:width], w_lo[:, slot, k, 0:width]
                        pe.matmul(dst, a_hi, b_hi, start=first and k == 0, stop=False)
                        pe.matmul(dst, a_hi, b_lo, start=False, stop=False)
                        ins = pe.matmul(dst, a_lo, b_hi, start=False, stop=last and k == kts - 1)
                ins.then_inc(chunk_used, 1)

            def column_chunk(at, t, j, s, free, width=NC_, h_from=None):
                if j == 0:
                    for f in free:
                        pe.wait_ge(*f)
                if h_from is not None:
                    pe.wait_ge(h_made, h_from + 2 * j + 2)
                chunk(at, t, h_hi, h_lo, 2 * j, s, j == 0, j == KT // 2 - 1, width=width)

            def slab_chunk(at, t, j, s, free, hi=slab_hi, lo=slab_lo):
                if j % 2 == 0:
                    for f in free:
                        pe.wait_ge(*f)
                chunk(at, t, hi, lo, j % 2 * 2, s, j % 2 == 0, j % 2 == 1)

            def turn(made, free):
                pe.wait_ge(*made)
                for f in free:
                    pe.wait_ge(*f)
                for b in range(BLK):
                    for j in range(QUAD):
                        ins = pe.transpose(tp[b][:, j * P:(j + 1) * P], stage[:, b, j * P:(j + 1) * P], ident[:])
                ins.then_inc(stage_turned, 1)

            def qk_product(a, j):
                if j < 2:
                    pe.wait_ge(qk_made, 4 * a + 4)
                else:
                    pe.wait_ge(biased, 4 * a + j - 1)
                dst = tp[j % 2]
                pe.matmul(dst[:, 0:P], qk[:, 0, j, 0:P], qk[:, 1, j, 0:P], start=True, stop=True)
                pe.matmul(dst[:, P:SKEW], qk[:, 0, j, P:SEQ], qk[:, 1, j, :], start=True, stop=True) \
                    .then_inc(scored, 1)

            def prob_turn(a, j):
                pe.wait_ge(exp_made, 8 * a + 2 * j + 2)
                if j:
                    pe.wait_ge(prob_t_made, 4 * a + j)
                for n in range(3):
                    cols = slice(n * P, (n + 1) * P)
                    ins = pe.transpose(pt[:, cols], prob[j % 2][:, cols], ident[:])
                ins.then_inc(prob_turned, 1)

            def pv_product(a, j):
                pe.wait_ge(prob_t_made, 4 * a + j + 1)
                pe.wait_ge(v_made, 2 * a + 2)
                if j:
                    pe.wait_ge(u_made, 4 * a + j)
                cols = slice(j * HD, (j + 1) * HD)
                pe.matmul(po[:, 0:P], prob_t[j % 2][:, 0:P], v[:, 0, cols], start=True, stop=True)
                pe.matmul(po[:, P:SEQ], prob_t[j % 2][:, P:2 * P], v[:, 0, cols], start=True, stop=False)
                pe.matmul(po[:, P:SEQ], prob_t[j % 2][:, 2 * P:SKEW], v[:, 1, cols], start=False, stop=True) \
                    .then_inc(pv_made, 1)

            def attend(a, t):
                if t == -1:
                    qk_product(a, 0)
                    qk_product(a, 1)
                if t in (3, 5, 7, 9):
                    pv_product(a, (t - 3) // 2)
                if t in (1, 3, 5, 7):
                    prob_turn(a, (t - 1) // 2)
                if t in (2, 4):
                    qk_product(a, 2 + (t - 2) // 2)

            def quad_chunk(at, i, t, q_free, q_tp_free):
                if t < 8:
                    column_chunk(at, t, t, 1, q_free)
                elif t < 16:
                    column_chunk(at, t, t - 8, 0, [(stage_made, 4 * i + 4)])
                else:
                    column_chunk(at, t, t - 16, 1, [(stage_made, 4 * i + 6)])
                if t == 10:
                    turn((stage_made, 2 * (FILL_Q0 + 2 * i) + 2), q_tp_free)
                if t == 18:
                    turn((stage_made, 2 * (FILL_K0 + 2 * i) + 2), [(qk_made, 4 * i + 2)])

            def turn_rows(which, q, free):
                for f in free:
                    pe.wait_ge(*f)
                if q >= 2:
                    pe.wait_ge(h_made, KT * which + 4 * (q - 1))
                for k in range(4 * q, 4 * q + 4):
                    for b in range(BLK):
                        ins = pe.transpose(four[k // 2 % 4][:, k % 2 * SEQ + b * P:k % 2 * SEQ + (b + 1) * P],
                                           xs[:, b, k * P:(k + 1) * P], ident[:])
                    ins.then_inc(h_turned, 1)

            pe.wait_ge(g_loaded, 32)
            pe.wait_ge(ident_made, 1)
            pe.transpose(acc[0][0][:, 0:2 * KT], g_rows[:], ident[0:2 * KT, 0:2 * KT]).then_inc(g_turned, 1)
            turn_rows(0, 0, [(x_loaded[0], 16)])

            for t in range(IDX_LEN):
                if t < 8:
                    column_chunk(IDX_AT, t, t, 0, [(g_out, 1)], h_from=0)
                elif t < 16:
                    column_chunk(IDX_AT, t, t - 8, 1, [], width=KIW)
                else:
                    column_chunk(IDX_AT, t, t - 16, 0, [(stage_made, 2)])
                if t in (0, 2, 4):
                    turn_rows(0, 1 + t // 2, [(x_loaded[1 + t // 2], 16)])
                if t == 9:
                    turn((stage_made, 2), [(h_made, KT)])
                if t in (10, 11, 18, 19):
                    g = (10, 11, 18, 19).index(t)
                    n = 4 if g < 3 else 8
                    if g == 0:
                        pe.wait_ge(hot_loaded, 16)
                        pe.wait_ge(rel_loaded, 16)
                        pe.wait_ge(rel_masked, 1)
                    if g >= 2:
                        pe.wait_ge(bias_rows_out, g - 1)
                    pe.matmul(dots[g % 2][0:n, 0:SKEW], rel[:, 4 * g:4 * g + n], hot[:, g, :],
                              start=True, stop=True).then_inc(bias_rows_made, 1)
                if t == 17:
                    pe.wait_ge(ki_made, 4)
                    pe.wait_ge(qi_t_made, 2)
                    for b in range(BLK):
                        ins = pe.transpose(tp[b][:, 0:P], ki_twice[:, b, :], ident[:])
                    ins.then_inc(ki_turned, 1)

            for t in range(QUAD_LEN):
                quad_chunk(QUAD_AT, 0, t, [(w_idx_made, 2)], [(qi_t_made, 4)])
                if t == 1:
                    turn((stage_made, 4), [(ki_t_made, 2)])
                if 2 <= t < 2 + N_IDX:
                    h = t - 2
                    pe.wait_ge(qi_t_made, 2 if h < 8 else 4)
                    if h == 0:
                        pe.wait_ge(bias_rows_out, 4)
                    if h >= 2:
                        pe.wait_ge(relu_made, h - 1)
                    half = slice(h % 2 * IDX, (h % 2 + 1) * IDX)
                    pe.matmul(dots[h % 2][:, 0:P], qi_t[half, h // 2, 0:P], ki_t[half, 0:P], start=True, stop=True)
                    pe.matmul(dots[h % 2][:, P:SKEW], qi_t[half, h // 2, P:SEQ], ki_t[half, :],
                              start=True, stop=True).then_inc(dots_made, 1)

            pe.wait_ge(relu_made, N_IDX)
            with pe.Fori(1, N_QUAD) as i:
                at = QUAD_AT + QUAD_LEN * i
                attend(i - 1, -1)
                for t in range(QUAD_LEN):
                    quad_chunk(at, i, t, [(v_made, 2 * i)], [(biased, 4 * i)])
                    attend(i - 1, t)

            def y_chunk(at, t, t0, s, kts, k0, free):
                j = t - t0
                if j == 0:
                    for f in free:
                        pe.wait_ge(*f)
                chunk(at, t, y_hi, y_lo, k0 + sum(kts[:j]), s, j == 0, j == len(kts) - 1, kts[j])

            attend(N_QUAD - 1, -1)
            for t in range(MERGE3_LEN):
                if t < 8:
                    column_chunk(MERGE0_AT, t, t, 0, [(stage_made, 2 * (FILL_K0 + 2 * N_QUAD - 1))])
                elif t < 16:
                    column_chunk(MERGE0_AT, t, t - 8, 1, [(v_made, 2 * N_QUAD)])
                elif t < 19:
                    y_chunk(MERGE0_AT, t, 16, 0, YA_KTS, 0, [(sig_made, 2), (y_made, 2)])
                else:
                    y_chunk(MERGE0_AT, t, 19, 1, YB_KTS, QUAD, [(sig_made, 4), (y_made, 6)])
                attend(N_QUAD - 1, t)
                if t == 12:
                    turn((stage_made, 2 * FILL_Y + 2), [(biased, N_HEADS)])
                if t in (14, 16):
                    n = (t - 12) // 2
                    turn((stage_made, 2 * (FILL_Y + n) + 2), [(y_made, 2 * n)])
            with pe.Fori(1, N_OUT - 1) as n:
                at = (MERGE_AT - MERGE_LEN) + MERGE_LEN * n
                added = 2 * N_OUT * n - 2 * N_OUT
                w_free = ((gated_b, 2 * n), (sig_made, 4 * n + 2), (x_added, added + 2), (x_added, added + 4))
                for t in range(MERGE_LEN):
                    if t < 8:
                        column_chunk(at, t, t, 0, [(gated_a, 2 * n)])
                    elif t < 16:
                        if t == 8:
                            pe.wait_ge(slab_made, 2 * n)
                        slab_chunk(at, t, t - 8, (t - 6) // 2 % 2, [w_free[(t - 8) // 2]])
                    elif t < 24:
                        column_chunk(at, t, t - 16, 1, [(x_added, added + 6)])
                    elif t < 27:
                        y_chunk(at, t, 24, 0, YA_KTS, 0, [(x_added, added + 8)])
                    else:
                        y_chunk(at, t, 27, 1, YB_KTS, QUAD, [(sig_made, 4 * n + 4)])
                    if t == 2:
                        turn((merged, n), [(y_made, 6)])
            n = N_OUT - 1
            for t in range(MERGE3_LEN):
                if t < 8:
                    column_chunk(MERGE3_AT, t, t, 0, [(gated_a, 2 * n)])
                elif t < 16:
                    column_chunk(MERGE3_AT, t, t - 8, 1, [(gated_b, 2 * n)])
                elif t < 19:
                    y_chunk(MERGE3_AT, t, 16, 0, YA_KTS, 0, [(sig_made, 4 * n + 2)])
                else:
                    y_chunk(MERGE3_AT, t, 19, 1, YB_KTS, QUAD, [(sig_made, 4 * n + 4)])
                if t == 2:
                    turn((merged, n), [(slab_made, 2 * (n - 1))])

            def last_slabs(at, t, before, before2, made):
                w_free = (*before2, *((x_added, before + n) for n in range(2, 14, 2)))[t // 2]
                if t % 8 == 0:
                    pe.wait_ge(slab_made, made + 2 * (t // 8))
                x_hi, x_lo = ((slab_hi, slab_lo), (y_hi, y_lo))[t // 8]
                slab_chunk(at, t, t % 8, t // 2 % 2, [w_free], x_hi, x_lo)

            for t in range(WOUT_LEN):
                last_slabs(WOUT_AT, t, 2 * N_OUT * (N_OUT - 2), ((gated_a, 2 * N_OUT), (gated_b, 2 * N_OUT)),
                           2 * (N_OUT - 1))
                if t == 2:
                    turn((merged, N_OUT), [(slab_made, 2 * (N_OUT - 1))])
                if t in (11, 13, 15):
                    q = (t - 11) // 2
                    turn_rows(1, q, [(x_added, 2 * N_OUT * (N_OUT - 1) + 2 * q + 2),
                                     *([(slab_made, 2 * N_OUT)], [(prob_t_made, N_HEADS), (u_made, N_HEADS)], [])[q]])

            added0 = 2 * N_OUT * N_OUT
            for t in range(FFN0_LEN):
                column_chunk(FFN0_AT, t, t % 8, t // 8, [(x_added, added0 - 2 + 2 * (t // 8))],
                             h_from=KT if t < 8 else None)
                if t == 1:
                    turn_rows(1, 3, [(x_added, added0)])
            with pe.Fori(1, N_SLAB - 1) as i:
                at = (FFN_AT - FFN_LEN) + FFN_LEN * i
                added = (added0 - 2 * N_OUT) + 2 * N_OUT * i
                w_free = ((swiglu_made, 2 * i), (silu_made, 2 * i + 2), (x_added, added + 2), (x_added, added + 4))
                for t in range(FFN_LEN):
                    if t < 8:
                        column_chunk(at, t, t, 0, [(x_added, added), (silu_made, 2 * i)])
                    elif t < 16:
                        if t == 8:
                            pe.wait_ge(slab_made, 2 * N_OUT + 2 * i)
                        slab_chunk(at, t, t - 8, (t - 6) // 2 % 2, [w_free[(t - 8) // 2]])
                    else:
                        column_chunk(at, t, t - 16, 1, [(x_added, added + 6)])
                    if t == 2:
                        turn((swiglu_made, 2 * i), [(slab_made, 2 * (N_OUT - 1) + 2 * i), (h_made, 2 * KT)])
            i = N_SLAB - 1
            before = added0 + 2 * N_OUT * (N_SLAB - 2)
            for t in range(FFN0_LEN):
                column_chunk(FFN10_AT, t, t % 8, t // 8, [(x_added, before) if t < 8 else (swiglu_made, 2 * i)])
                if t == 2:
                    turn((swiglu_made, 2 * i), [(slab_made, 2 * (N_OUT - 1) + 2 * i)])
            for t in range(DOWN_LEN):
                last_slabs(DOWN_AT, t, before, ((silu_made, 2 * N_SLAB), (swiglu_made, 2 * N_SLAB)),
                           2 * (N_OUT + N_SLAB - 1))
                if t == 2:
                    turn((swiglu_made, 2 * N_SLAB), [(slab_made, 2 * (N_OUT + N_SLAB - 1))])


def bucket_rows():
    dist = SEQ - 1 - np.arange(SKEW)
    far = np.maximum(dist, 1).astype(np.float32) / np.float32(BUCKETS // 2)
    large = BUCKETS // 2 + (np.log(far) / np.float32(np.log(2048 / (BUCKETS // 2)))
                            * np.float32(BUCKETS // 2)).astype(np.int32)
    bucket = np.where(dist < BUCKETS // 2, np.maximum(dist, 0), np.minimum(large, BUCKETS - 1))
    rows = np.zeros((BUCKETS + 1, 4, SKEW), np.float32)
    for g, (window, dilation) in enumerate(((128, 1), (512, 4), (2048, 16), (SEQ, 1))):
        seen = (dist >= 0) & (dist <= window) & (dist % dilation == 0)
        rows[np.where(seen, bucket, BUCKETS), g, np.arange(SKEW)] = 1.0
    return rows


_INS = ("x", "w_in", "w_out_a", "w_out_b", "w_out", "w_ff_gate", "w_ff_up", "w_ff_down", "g_mix", "g_ffn",
        "g_final", "rel_bias")


def kernel(**inputs):
    import concourse.bacc as bacc
    from concourse.bass_utils import run_bass_kernel_spmd

    nc = bacc.Bacc("TRN2", target_bir_lowering=False, num_devices=1)
    f32 = mybir.dt.float32
    arrays = {f"in_{name}": np.ascontiguousarray(inputs[name]) for name in _INS}
    arrays["in_onehot"] = bucket_rows()
    args = [nc.dram_tensor(name, a.shape, f32, kind="ExternalInput").ap() for name, a in arrays.items()]
    out = nc.dram_tensor("out", (1, SEQ, D), f32, kind="ExternalOutput").ap()
    bias_rows = nc.dram_tensor("bias_rows", (N_HEADS, P * (SKEW + 1)), f32, kind="Internal").ap()
    build(nc, *args, out, bias_rows)
    r = run_bass_kernel_spmd(nc, [arrays], core_ids=[0])
    return r.results[0]["out"]
```

```python
import concourse.bass as bass
from concourse import mybir
from contextlib import ExitStack
import numpy as np

P = 128
SEQ = 256
BLK = SEQ // P
D = 2048
KT = D // P
HD = 128
N_GROUP_A, QUAD = 3, 4
N_QUAD_B = 2
N_QUAD = N_GROUP_A + N_QUAD_B
QW = QUAD * HD
WIDTH_A = N_GROUP_A * QW
WIDTH_B = N_QUAD_B * QW
N_IDX, IDX = 16, 64
D_FF = 5632
BUCKETS = 32
N_HEADS = N_QUAD * QUAD
TOPK = 64
EPS = 1e-6
NEG = -1e30
TAKEN = -3e38
COL_Q_A, COL_K_A, COL_V_A = 0, WIDTH_A, 2 * WIDTH_A
COL_Q_B = 3 * WIDTH_A
COL_K_B, COL_V_B = COL_Q_B + WIDTH_B, COL_Q_B + 2 * WIDTH_B
COL_QI = COL_Q_B + 3 * WIDTH_B
COL_KI = COL_QI + N_IDX * IDX
KIW = IDX + N_IDX
COL_GA = COL_KI + KIW
COL_GB = COL_GA + D
NC_ = 512
N_OUT = D // NC_
N_SLAB = D_FF // NC_
SKEW = 3 * P
RING = 4
AHEAD = RING - 1

IDX_AT, IDX_LEN = 0, 24
QUAD_AT, QUAD_LEN = 24, 24
MERGE0_AT = QUAD_AT + N_QUAD * QUAD_LEN
MERGE_AT, MERGE_LEN = MERGE0_AT + 24, 32
MERGE3_AT, MERGE3_LEN = MERGE_AT + (N_OUT - 2) * MERGE_LEN, 24
WOUT_AT, WOUT_LEN = MERGE3_AT + MERGE3_LEN, 16
FFN0_AT, FFN0_LEN = WOUT_AT + WOUT_LEN, 16
FFN_AT, FFN_LEN = FFN0_AT + FFN0_LEN, 24
FFN10_AT = FFN_AT + (N_SLAB - 2) * FFN_LEN
DOWN_AT, DOWN_LEN = FFN10_AT + FFN0_LEN, 16
YA_KTS = (2, 1, 1)
YB_KTS = (2, 2, 2, 1, 1)
MERGE3_KTS = (2,) * 16 + YA_KTS + YB_KTS
MERGE_KTS = (2,) * 24 + YA_KTS + YB_KTS


def build(nc, x, w_in, w_out_a, w_out_b, w_out, w_gate, w_up, w_down, g_mix, g_ffn, g_final,
          rel_bias, onehot, out, bias_rows):
    f32, f32r = mybir.dt.float32, mybir.dt.float32r
    ACT, ALU, AX = mybir.ActivationFunctionType, mybir.AluOpType, mybir.AxisListType
    w_in, w_out_a, w_out_b, w_out = w_in[0], w_out_a[0], w_out_b[0], w_out[0]
    w_gate, w_up, w_down = w_gate[0], w_up[0], w_down[0]

    ctx = ExitStack()
    with ctx:
        def sb(name, shape, dt=f32):
            return ctx.enter_context(nc.sbuf_tensor(name, shape, dt))

        def sem(name):
            return ctx.enter_context(nc.semaphore(name))

        xs = sb("xs", [P, BLK, D])
        h_hi = sb("h_hi", [P, KT, SEQ], f32r)
        h_lo = sb("h_lo", [P, KT, SEQ], f32r)
        raw = sb("raw", [P, RING, 2, NC_])
        w_hi = sb("w_hi", [P, RING, 2, NC_], f32r)
        w_lo = sb("w_lo", [P, RING, 2, NC_], f32r)
        bias = sb("bias", [P, N_HEADS, SKEW])
        u = sb("u", [P, N_QUAD, BLK, QW])
        y_hi = sb("y_hi", [P, 3 * QUAD, SEQ], f32r)
        y_lo = sb("y_lo", [P, 3 * QUAD, SEQ], f32r)
        slab_hi = sb("slab_hi", [P, QUAD, SEQ], f32r)
        slab_lo = sb("slab_lo", [P, QUAD, SEQ], f32r)
        stage = sb("stage", [P, BLK, QW])
        qk = sb("qk", [P, 2, QUAD, SEQ])
        v = sb("v", [P, BLK, QW])
        att = sb("att", [P, 6, SKEW])
        score = [att[:, j, :] for j in range(2)]
        prob = [att[:, 2 + j, :] for j in range(2)]
        prob_t = [att[:, 4 + j, :] for j in range(2)]
        ident = sb("ident", [P, P])
        g_rows = [sb(f"g_rows{n}", [KT, P]) for n in range(2)]
        g_cols = sb("g_cols", [P, 2 * KT])
        rel = sb("rel", [BUCKETS + 1, N_HEADS])
        neg_max = sb("neg_max", [P, N_QUAD, BLK * QUAD])
        denom = sb("denom", [P, N_QUAD, BLK * QUAD])
        mix = sb("mix", [P, 8, BLK * QUAD])
        sq = sb("sq", [P, 3, BLK, N_OUT])
        norm = sb("norm", [P, 3, 7, BLK])
        inv_rms = norm[:, :, 6, :]
        warm = sb("warm", [P, 2])
        top = sb("top", [P, BLK, 8])
        w_idx = sb("w_idx", [P, BLK, N_IDX])
        flat_u = u[:].rearrange("p a b n -> p (a b n)")
        xg = flat_u[:, 0:BLK * D].rearrange("p (b n) -> p b n", b=BLK)
        qi_t = flat_u[:, 0:2048].rearrange("p (t s) -> p t s", t=8)
        ki_t = flat_u[:, 2048:2304]
        ki_twice = flat_u[:, 2304:2560].rearrange("p (b n) -> p b n", b=BLK)
        relu = [flat_u[:, 2560 + SKEW * j:2560 + SKEW * (j + 1)] for j in range(2)]
        ki_cols = flat_u[0:KIW, 3328:3584]
        idx_score = flat_u[:, BLK * D:BLK * D + SKEW]
        idx_left = flat_u[:, BLK * D + SKEW:BLK * D + 2 * SKEW]
        hot = qk[0:BUCKETS + 1].rearrange("p a j s -> p (a j s)")[:, 0:4 * SKEW] \
            .rearrange("p (g m) -> p g m", g=4)
        rows_sb = att[0:8, 0:4, :]
        sig_a, sig_b = [qk[:, i, :, :].rearrange("p j s -> p (j s)")
                        .rearrange("p (b n) -> p b n", b=BLK) for i in range(2)]
        silu = sig_a
        spare = v
        g_last = bias[:].rearrange("p h m -> p (h m)")[:, 0:D]

        acc = [[ctx.enter_context(nc.psum_tensor(f"acc{s}{b}", [P, NC_], f32)) for b in range(BLK)]
               for s in range(2)]
        tp = [ctx.enter_context(nc.psum_tensor(f"tp{b}", [P, NC_], f32)) for b in range(2)]
        pt = ctx.enter_context(nc.psum_tensor("pt", [P, NC_], f32))
        po = ctx.enter_context(nc.psum_tensor("po", [P, NC_], f32))
        four = [tp[0], tp[1], pt, po]
        dots = [pt, po]

        x_loaded = [sem(f"x_loaded{q}") for q in range(N_OUT)]
        raw_loaded = [sem(f"raw_loaded{s}") for s in range(RING)]
        g_mix_loaded, g_ffn_loaded, g_last_loaded = sem("g_mix_loaded"), sem("g_ffn_loaded"), sem("g_last_loaded")
        hot_loaded, rel_loaded, rel_masked = sem("hot_loaded"), sem("rel_loaded"), sem("rel_masked")
        ident_zero, ident_made = sem("ident_zero"), sem("ident_made")
        idx_zero, warm_made = sem("idx_zero"), sem("warm_made")
        bias_rows_made, bias_rows_out = sem("bias_rows_made"), sem("bias_rows_out")
        bias_rows_stored = sem("bias_rows_stored")
        bias_loaded, bias_step, bias_chosen = sem("bias_loaded"), sem("bias_step"), sem("bias_chosen")
        g_turned, g_out = sem("g_turned"), sem("g_out")
        squares, mean_made = sem("squares"), sem("mean_made")
        root_made, scale_made = sem("root_made"), sem("scale_made")
        norm_step = sem("norm_step")
        h_turned, h_hi_made, h_made = sem("h_turned"), sem("h_hi_made"), sem("h_made")
        hi_made, lo_made, chunk_used = sem("hi_made"), sem("lo_made"), sem("chunk_used")
        stage_made, stage_turned, part_hi = sem("stage_made"), sem("stage_turned"), sem("part_hi")
        y_made, slab_made = sem("y_made"), sem("slab_made")
        qi_t_made, ki_cols_made, ki_rows_turned = sem("qi_t_made"), sem("ki_cols_made"), sem("ki_rows_turned")
        ki_made, w_idx_made = sem("ki_made"), sem("w_idx_made")
        ki_turned, ki_t_made = sem("ki_turned"), sem("ki_t_made")
        dots_made, relu_made = sem("dots_made"), sem("relu_made")
        idx_added, top_step = sem("idx_added"), sem("top_step")
        qk_made, v_made = sem("qk_made"), sem("v_made")
        scored, biased, max_made, exp_made = sem("scored"), sem("biased"), sem("max_made"), sem("exp_made")
        prob_turned, prob_t_made = sem("prob_turned"), sem("prob_t_made")
        pv_made, u_made = sem("pv_made"), sem("u_made")
        mix_in, mix_exp, mix_step = sem("mix_in"), sem("mix_exp"), sem("mix_step")
        sig_made, gated_a, gated_b, merged = sem("sig_made"), sem("gated_a"), sem("gated_b"), sem("merged")
        silu_made, swiglu_made, x_added = sem("silu_made"), sem("swiglu_made"), sem("x_added")
        last_made, xg_made = sem("last_made"), sem("xg_made")
        out_left_made, out_right_made, out_stored = sem("out_left_made"), sem("out_right_made"), sem("out_stored")

        FILL_QI = (0, 1)
        FILL_Q0, FILL_K0 = 2, 3
        FILL_Y = 2 + 2 * N_QUAD
        FILL_SLAB = FILL_Y + 3

        block = ctx.enter_context(nc.Block())

        @block.sync
        def _(sp):
            def load(at, t, src):
                slot, c = t % RING, at + t
                if not (isinstance(at, int) and c < RING):
                    sp.wait_ge(lo_made, c - RING + 1)
                kts, width = src.shape[0] // P, src.shape[1]
                sp.dma_start(raw[:, slot, 0:kts, 0:width], src.rearrange("(t p) n -> p t n", p=P)) \
                    .then_inc(raw_loaded[slot], 16)

            def column(at, t0, w, col, width=NC_):
                for k in range(KT // 2):
                    load(at, t0 + k, w[2 * k * P:2 * (k + 1) * P, bass.ds(col, width)])

            def row_slab(at, t0, w, row):
                for n in range(N_OUT):
                    for k in range(2):
                        load(at, t0 + 2 * n + k, w[bass.ds(row + 2 * k * P, 2 * P), n * NC_:(n + 1) * NC_])

            def outs(at, t0, col):
                t = t0
                for w, kts in ((w_out_a, YA_KTS), (w_out_b, YB_KTS)):
                    row = 0
                    for k in kts:
                        load(at, t, w[row:row + k * P, bass.ds(col, NC_)])
                        row, t = row + k * P, t + 1

            def load_x(q):
                cols = slice(q * NC_, (q + 1) * NC_)
                sp.dma_start(xs[:, :, cols], x[0, :, cols].rearrange("(b p) n -> p b n", p=P)) \
                    .then_inc(x_loaded[q], 16)

            load_x(0)
            for k in range(KT // 2):
                load(IDX_AT, k, w_in[2 * k * P:2 * (k + 1) * P, COL_QI:COL_QI + NC_])
                if 1 <= k < N_OUT:
                    load_x(k)
            column(IDX_AT, 8, w_in, COL_KI, KIW)
            column(IDX_AT, 16, w_in, COL_QI + NC_)
            with sp.Fori(0, N_GROUP_A) as i:
                for n, col in enumerate((COL_Q_A, COL_K_A, COL_V_A)):
                    column(QUAD_AT + QUAD_LEN * i, 8 * n, w_in, col + QW * i)
            with sp.Fori(0, N_QUAD_B) as i:
                for n, col in enumerate((COL_Q_B, COL_K_B, COL_V_B)):
                    column(QUAD_AT + N_GROUP_A * QUAD_LEN + QUAD_LEN * i, 8 * n, w_in, col + QW * i)
            column(MERGE0_AT, 0, w_in, COL_GA)
            column(MERGE0_AT, 8, w_in, COL_GB)
            outs(MERGE0_AT, 16, 0)
            with sp.Fori(0, N_OUT - 2) as n:
                at = MERGE_AT + MERGE_LEN * n
                column(at, 0, w_in, COL_GA + NC_ + NC_ * n)
                row_slab(at, 8, w_out, NC_ * n)
                column(at, 16, w_in, COL_GB + NC_ + NC_ * n)
                outs(at, 24, NC_ + NC_ * n)
            column(MERGE3_AT, 0, w_in, COL_GA + (N_OUT - 1) * NC_)
            column(MERGE3_AT, 8, w_in, COL_GB + (N_OUT - 1) * NC_)
            outs(MERGE3_AT, 16, (N_OUT - 1) * NC_)
            for s in range(2):
                row_slab(WOUT_AT, 8 * s, w_out, (N_OUT - 2 + s) * NC_)
            column(FFN0_AT, 0, w_gate, 0)
            column(FFN0_AT, 8, w_up, 0)
            with sp.Fori(1, N_SLAB - 1) as i:
                at = (FFN_AT - FFN_LEN) + FFN_LEN * i
                column(at, 0, w_gate, NC_ * i)
                row_slab(at, 8, w_down, NC_ * i - NC_)
                column(at, 16, w_up, NC_ * i)
            column(FFN10_AT, 0, w_gate, (N_SLAB - 1) * NC_)
            column(FFN10_AT, 8, w_up, (N_SLAB - 1) * NC_)
            for s in range(2):
                row_slab(DOWN_AT, 8 * s, w_down, (N_SLAB - 2 + s) * NC_)
            for b in range(BLK):
                for made, cols in ((out_left_made, slice(0, D // 2)), (out_right_made, slice(D // 2, D))):
                    sp.wait_ge(made, b + 1)
                    sp.dma_start(out[0, b * P:(b + 1) * P, cols], xg[:, b, cols]).then_inc(out_stored, 16)
            sp.wait_ge(out_stored, 16 * 2 * BLK)

        @block.gpsimd
        def _(pool):
            pool.memset(ident[:], 0.0).then_inc(ident_zero, 1)
            pool.wait_ge(ident_zero, 1)
            pool.affine_select(out=ident[:], in_=ident[:], compare_op=ALU.not_equal, fill=1.0, base=0,
                               pattern=[[-1, P]], channel_multiplier=1).then_inc(ident_made, 1)
            pool.dma_start(hot, onehot).then_inc(hot_loaded, 16)
            pool.dma_start(rel[0:BUCKETS, :], rel_bias).then_inc(rel_loaded, 16)
            pool.wait_ge(ident_made, 1)
            pool.memset(rel[BUCKETS:BUCKETS + 1, :], NEG).then_inc(rel_masked, 1)
            pool.wait_ge(rel_masked, 1)
            pool.memset(idx_score, 0.0).then_inc(idx_zero, 1)
            pool.wait_ge(idx_zero, 1)
            pool.affine_select(out=idx_score[:, 0:P], in_=idx_score[:, 0:P], compare_op=ALU.is_ge, fill=NEG,
                               base=0, pattern=[[-1, P]], channel_multiplier=1).then_inc(idx_zero, 1)
            pool.affine_select(out=idx_score[:, P:SKEW], in_=idx_score[:, P:SKEW], compare_op=ALU.is_ge,
                               fill=NEG, base=P, pattern=[[-1, SEQ]], channel_multiplier=1).then_inc(idx_zero, 1)
            for g in range(4):
                n = 4 if g < 3 else 8
                pool.wait_ge(bias_rows_out, g + 1)
                pool.dma_start(bias_rows[4 * g:4 * g + n].rearrange("h (q m) -> h q m", q=P)[:, :, 0:SKEW],
                               rows_sb[0:n, g, :].unsqueeze(1).to_broadcast([n, P, SKEW])) \
                    .then_inc(bias_rows_stored, 16)
            pool.wait_ge(bias_rows_stored, 4 * 16)
            for a in range(N_QUAD):
                skewed = bias_rows[4 * a:4 * a + QUAD, 0:P * SKEW].rearrange("h (q m) -> q h m", q=P)
                for lo, width, at in ((P, P, 0), (0, SEQ, P)):
                    src = bass.AP(skewed.tensor, skewed.offset + P - 1 + lo, [*skewed.ap[:2], [1, width]])
                    pool.dma_start(bias[:, 4 * a:4 * a + QUAD, at:at + width], src).then_inc(bias_loaded, 16)
            pool.wait_ge(bias_loaded, 2 * N_QUAD * 16)
            pool.wait_ge(top_step, 4 * TOPK // 8)
            pool.tensor_scalar(idx_left, idx_left, TAKEN / 2, NEG, ALU.is_gt, ALU.mult).then_inc(bias_step, 1)
            pool.wait_ge(bias_step, 1)
            for h in range(N_GROUP_A * QUAD, N_HEADS):
                pool.tensor_tensor(bias[:, h, :], bias[:, h, :], idx_left, ALU.add).then_inc(bias_chosen, 1)
            pool.wait_ge(biased, N_HEADS)
            pool.dma_start(g_last, g_final.partition_broadcast(P)).then_inc(g_last_loaded, 16)

        @block.scalar
        def _(act):
            def hi(at, t, turn, kts=2, width=NC_):
                slot = t % RING
                act.wait_ge(raw_loaded[slot], 16 * (turn + t // RING + 1))
                if not (isinstance(at, int) and at + t < RING):
                    act.wait_ge(chunk_used, at + t - RING + 1)
                act.activation(w_hi[:, slot, 0:kts, 0:width], raw[:, slot, 0:kts, 0:width], ACT.Copy) \
                    .then_inc(hi_made, 1)

            def copy_stage(last_chunk, s, fill):
                act.wait_ge(chunk_used, last_chunk + 1)
                act.wait_ge(stage_turned, fill)
                act.activation(stage[:, 0, :], acc[s][0][:], ACT.Copy, scale=inv_rms[:, 0, 0:1]).then_inc(stage_made, 1)

            def copy_turned(dst, fill, done):
                act.wait_ge(stage_turned, fill + 1)
                act.activation(dst[:, :, 0:P], tp[0][:].rearrange("p (j s) -> p j s", j=QUAD), ACT.Copy) \
                    .then_inc(done, 1)

            def hi_turned(dst, fill):
                act.wait_ge(stage_turned, fill + 1)
                for b in range(BLK):
                    act.activation(dst[:, :, b * P:(b + 1) * P], tp[b][:].rearrange("p (j s) -> p j s", j=QUAD),
                                   ACT.Copy).then_inc(part_hi, 1)

            def exps(a, j):
                act.wait_ge(max_made, 8 * a + 2 * j + 2)
                if j >= 2:
                    act.wait_ge(prob_turned, 4 * a + j - 1)
                for b, cols in ((0, slice(0, P)), (1, slice(P, SKEW))):
                    i = b * QUAD + j
                    act.activation(prob[j % 2][:, cols], score[j % 2][:, cols], ACT.Exp,
                                   bias=neg_max[:, a, i:i + 1], accum_out=denom[:, a, i:i + 1]) \
                        .then_inc(exp_made, 1)

            def copy_prob(a, j):
                act.wait_ge(prob_turned, 4 * a + j + 1)
                if j >= 2:
                    act.wait_ge(pv_made, 4 * a + j - 1)
                act.activation(prob_t[j % 2], pt[:, 0:SKEW], ACT.Copy).then_inc(prob_t_made, 1)

            def attend(a, t):
                if t in (-1, 0, 2, 4):
                    exps(a, (-1, 0, 2, 4).index(t))
                if t in (1, 3, 5, 7):
                    copy_prob(a, (1, 3, 5, 7).index(t))

            def quad(at, i, t):
                if t == 7:
                    copy_stage(at + 7, 1, FILL_Q0 + 2 * i)
                if t == 10:
                    copy_turned(qk[:, 0], FILL_Q0 + 2 * i, qk_made)
                if t == 15:
                    copy_stage(at + 15, 0, FILL_K0 + 2 * i)
                if t == 18:
                    copy_turned(qk[:, 1], FILL_K0 + 2 * i, qk_made)
                if t == 23:
                    act.wait_ge(chunk_used, at + 24)
                    act.activation(v[:, 0, :], acc[1][0][:], ACT.Copy, scale=inv_rms[:, 0, 0:1]).then_inc(v_made, 1)

            def gates(at, t, s, dst, before):
                act.wait_ge(chunk_used, at + t + 1)
                if before is not None:
                    act.wait_ge(*before)
                for b in range(BLK):
                    act.activation(dst[:, b, :], acc[s][b][:], ACT.Sigmoid, scale=inv_rms[:, 0, b:b + 1]) \
                        .then_inc(sig_made, 1)

            def square_part(which, n, before, blocks=range(BLK)):
                if which or before:
                    act.wait_ge(squares, 2 * N_OUT * which + before)
                for b in blocks:
                    act.activation(spare[:, b, :], xs[:, b, n * NC_:(n + 1) * NC_], ACT.Square,
                                   accum_out=sq[:, which, b, n:n + 1]).then_inc(squares, 1)

            def root(which, b=None):
                rows = slice(0, BLK) if b is None else slice(b, b + 1)
                act.wait_ge(mean_made, which + 1 + (b or 0))
                act.activation(norm[:, which, 1, rows], norm[:, which, 0, rows], ACT.Sqrt).then_inc(root_made, 1)

            def hi_rows(which, q, part=range(4)):
                for k in (4 * q + j for j in part):
                    act.wait_ge(h_turned, KT * which + k // 2 * 2 + 2)
                    act.activation(h_hi[:, k, :], four[k // 2 % 4][:, k % 2 * SEQ:(k % 2 + 1) * SEQ], ACT.Copy,
                                   scale=g_cols[:, KT * which + k:KT * which + k + 1]).then_inc(h_hi_made, 1)

            act.dma_start(g_rows[0][:], g_mix.rearrange("a (k p) -> (a k) p", p=P)).then_inc(g_mix_loaded, 16)
            act.dma_start(g_rows[1][:], g_ffn.rearrange("a (k p) -> (a k) p", p=P)).then_inc(g_ffn_loaded, 16)
            act.wait_ge(warm_made, 1)
            act.activation(warm[:, 1:2], warm[:, 0:1], ACT.Copy)
            act.wait_ge(g_out, 1)
            hi_rows(0, 0, (0, 1))
            hi(IDX_AT, 0, 0)
            hi_rows(0, 0, (2, 3))
            hi(IDX_AT, 1, 0)
            hi(IDX_AT, 2, 0)

            for t in range(IDX_LEN):
                hi(IDX_AT, t + AHEAD, 0, width=KIW if 8 <= t + AHEAD < 16 else NC_)
                if t in (0, 2, 4):
                    hi_rows(0, 1 + t // 2)
                if t < 4:
                    act.wait_ge(x_loaded[t], 16)
                    square_part(0, t, 2 * t)
                if t == 5:
                    root(0)
                if t == 7:
                    act.wait_ge(scale_made, 1)
                    copy_stage(IDX_AT + 7, 0, FILL_QI[0])
                if t == 9:
                    copy_turned(qi_t[:, 0:4], FILL_QI[0], qi_t_made)
                if t == 19:
                    act.wait_ge(ki_turned, 1)
                    act.activation(ki_t[:, 0:P], tp[0][:, 0:P], ACT.Copy).then_inc(ki_t_made, 1)
                if t == 23:
                    copy_stage(IDX_AT + 23, 0, FILL_QI[1])

            for t in range(QUAD_LEN):
                hi(QUAD_AT, t + AHEAD, QUAD_AT // RING)
                if t == 1:
                    copy_turned(qi_t[:, 4:8], FILL_QI[1], qi_t_made)
                if 2 <= t < 2 + N_IDX:
                    h = t - 2
                    act.wait_ge(dots_made, h + 1)
                    if h >= 2:
                        act.wait_ge(idx_added, 2 * (h - 1))
                    act.activation(relu[h % 2], dots[h % 2][:, 0:SKEW], ACT.Relu).then_inc(relu_made, 1)
                quad(QUAD_AT, 0, t)

            with act.Fori(1, N_QUAD) as i:
                at = QUAD_AT + QUAD_LEN * i
                attend(i - 1, -1)
                for t in range(QUAD_LEN):
                    hi(at, t + AHEAD, QUAD_AT // RING + QUAD_LEN // RING * i)
                    attend(i - 1, t)
                    quad(at, i, t)

            attend(N_QUAD - 1, -1)
            for t in range(MERGE3_LEN):
                nxt = t + AHEAD
                hi(MERGE0_AT, nxt, MERGE0_AT // RING, MERGE3_KTS[nxt] if nxt < MERGE3_LEN else 2)
                attend(N_QUAD - 1, t)
                if t == 8:
                    act.wait_ge(mix_in, 1)
                    act.activation(mix[:, 4:7, :], mix[:, 1:4, :], ACT.Exp).then_inc(mix_exp, 1)
                if t == 9:
                    gates(MERGE0_AT, 7, 0, sig_a, (scored, N_HEADS))
                if t in (13, 15, 17):
                    n = (t - 13) // 2
                    hi_turned(y_hi[:, QUAD * n:QUAD * (n + 1)], FILL_Y + n)
                if t == 16:
                    gates(MERGE0_AT, 15, 1, sig_b, None)
            with act.Fori(1, N_OUT - 1) as n:
                at = (MERGE_AT - MERGE_LEN) + MERGE_LEN * n
                turn = (MERGE_AT - MERGE_LEN) // RING + MERGE_LEN // RING * n
                for t in range(MERGE_LEN):
                    nxt = t + AHEAD
                    hi(at, nxt, turn, MERGE_KTS[nxt] if nxt < MERGE_LEN else 2)
                    if t == 2:
                        hi_turned(slab_hi[:], FILL_SLAB - 1 + n)
                    if t == 7:
                        gates(at, 7, 0, sig_a, (gated_a, 2 * n))
                    if t == 23:
                        gates(at, 23, 1, sig_b, (merged, n))
            for t in range(MERGE3_LEN):
                nxt = t + AHEAD
                hi(MERGE3_AT, nxt, MERGE3_AT // RING, MERGE3_KTS[nxt] if nxt < MERGE3_LEN else 2)
                if t == 2:
                    hi_turned(slab_hi[:], FILL_SLAB + N_OUT - 2)
                if t == 7:
                    gates(MERGE3_AT, 7, 0, sig_a, (gated_a, 2 * (N_OUT - 1)))
                if t == 15:
                    gates(MERGE3_AT, 15, 1, sig_b, (merged, N_OUT - 1))
            act.wait_ge(g_out, 2)
            for t in range(WOUT_LEN):
                hi(WOUT_AT, t + AHEAD, WOUT_AT // RING)
                if t == 2:
                    hi_turned(y_hi[:, 0:QUAD], FILL_SLAB + N_OUT - 1)
                if t in (9, 11, 13, 15):
                    act.wait_ge(x_added, 2 * N_OUT * (N_OUT - 1) + t - 7)
                    square_part(1, (t - 9) // 2, t - 9)
                if t in (11, 13, 15):
                    hi_rows(1, (t - 11) // 2)

            def silu_gate(at, i):
                act.wait_ge(chunk_used, at + 8)
                for b in range(BLK):
                    act.activation(silu[:, b, :], acc[0][b][:], ACT.Silu, scale=inv_rms[:, 1, b:b + 1]) \
                        .then_inc(silu_made, 1)

            for t in range(FFN0_LEN):
                hi(FFN0_AT, t + AHEAD, FFN0_AT // RING)
                if t == 1:
                    hi_rows(1, 3)
                if t == 2:
                    root(1)
                if t == 7:
                    act.wait_ge(scale_made, 2)
                    silu_gate(FFN0_AT, 0)
            with act.Fori(1, N_SLAB - 1) as i:
                at = (FFN_AT - FFN_LEN) + FFN_LEN * i
                for t in range(FFN_LEN):
                    hi(at, t + AHEAD, (FFN_AT - FFN_LEN) // RING + FFN_LEN // RING * i)
                    if t == 2:
                        hi_turned(slab_hi[:], FILL_SLAB + N_OUT - 1 + i)
                    if t == 7:
                        silu_gate(at, i)
            for t in range(FFN0_LEN):
                hi(FFN10_AT, t + AHEAD, FFN10_AT // RING)
                if t == 2:
                    hi_turned(slab_hi[:], FILL_SLAB + N_OUT + N_SLAB - 2)
                if t == 7:
                    silu_gate(FFN10_AT, N_SLAB - 1)
            for t in range(DOWN_LEN):
                if t + AHEAD < DOWN_LEN:
                    hi(DOWN_AT, t + AHEAD, DOWN_AT // RING)
                if t == 2:
                    hi_turned(y_hi[:, 0:QUAD], FILL_SLAB + N_OUT + N_SLAB - 1)
                if t == 4:
                    act.activation(norm[:, 2, 1, :], norm[:, 1, 0, :], ACT.Sqrt)
                if t in (10, 12):
                    act.wait_ge(x_added, 2 * N_OUT * (N_OUT + N_SLAB - 1) + t - 8)
                    square_part(2, (t - 10) // 2, t - 10)
            for b in range(BLK):
                for s in range(2):
                    n = 2 * b + s
                    act.wait_ge(x_added, 2 * N_OUT * (N_OUT + N_SLAB) - 2 * BLK + n + 1)
                    square_part(2, N_OUT - 2 + s, 2 * (N_OUT - 2) + n, [b])
                root(2, b)
                act.wait_ge(scale_made, 3 + b)
                act.wait_ge(xg_made, 2 * (N_OUT - 2) + 2 * (b + 1))
                act.activation(xg[:, b, D // 2:D], xg[:, b, D // 2:D], ACT.Copy, scale=inv_rms[:, 2, b:b + 1]) \
                    .then_inc(out_right_made, 1)

        @block.vector
        def _(dve):
            class Chain:

                def __init__(self, s):
                    self.s, self.n = s, 0

                def then(self, ins):
                    self.n += 1
                    ins.then_inc(self.s, 1)
                    dve.wait_ge(self.s, self.n)

            def lo(at, t, kts=2, width=NC_):
                slot = t % RING
                dve.wait_ge(hi_made, at + t + 1)
                dve.tensor_tensor(w_lo[:, slot, 0:kts, 0:width], raw[:, slot, 0:kts, 0:width],
                                  w_hi[:, slot, 0:kts, 0:width].bitcast(f32), ALU.subtract).then_inc(lo_made, 1)

            def copy_stage(last_chunk, s, fill):
                dve.wait_ge(chunk_used, last_chunk + 1)
                dve.wait_ge(stage_turned, fill)
                dve.tensor_scalar(stage[:, 1, :], acc[s][1][:], inv_rms[:, 0, 1:2], None, ALU.mult) \
                    .then_inc(stage_made, 1)

            def copy_turned(dst, fill, done):
                dve.wait_ge(stage_turned, fill + 1)
                dve.tensor_copy(dst[:, :, P:SEQ], tp[1][:].rearrange("p (j s) -> p j s", j=QUAD)).then_inc(done, 1)

            def lo_turned(dst, of, fill, done):
                for b in range(BLK):
                    dve.wait_ge(part_hi, 2 * (fill - FILL_Y) + b + 1)
                    cols = slice(b * P, (b + 1) * P)
                    dve.tensor_tensor(dst[:, :, cols], tp[b][:].rearrange("p (j s) -> p j s", j=QUAD),
                                      of[:, :, cols].bitcast(f32), ALU.subtract).then_inc(done, 1)

            def scores(a, j):
                dve.wait_ge(scored, 4 * a + j + 1)
                if j >= 2:
                    dve.wait_ge(exp_made, 8 * a + 2 * (j - 1))
                dve.scalar_tensor_tensor(out=score[j % 2], in0=tp[j % 2][:, 0:SKEW], scalar=HD ** -0.5,
                                         in1=bias[:, 4 * a + j, :], op0=ALU.mult, op1=ALU.add).then_inc(biased, 1)
                dve.wait_ge(biased, 4 * a + j + 1)
                for b, cols in ((0, slice(0, P)), (1, slice(P, SKEW))):
                    i = b * QUAD + j
                    dve.tensor_reduce(neg_max[:, a, i:i + 1], score[j % 2][:, cols], AX.X, ALU.max,
                                      negate=True).then_inc(max_made, 1)

            def copy_out(a, j):
                dve.wait_ge(pv_made, 4 * a + j + 1)
                dve.tensor_copy(u[:, a, :, j * HD:(j + 1) * HD],
                                po[:, 0:SEQ].rearrange("p (b d) -> p b d", b=BLK)).then_inc(u_made, 1)

            def attend(a, t):
                if t == -1:
                    scores(a, 0)
                    scores(a, 1)
                if t in (2, 4):
                    scores(a, 2 + (t - 2) // 2)
                if t in (3, 5, 7, 9):
                    copy_out(a, (t - 3) // 2)

            def quad(at, i, t):
                if t == 7:
                    copy_stage(at + 7, 1, FILL_Q0 + 2 * i)
                if t == 10:
                    copy_turned(qk[:, 0], FILL_Q0 + 2 * i, qk_made)
                if t == 15:
                    copy_stage(at + 15, 0, FILL_K0 + 2 * i)
                if t == 18:
                    copy_turned(qk[:, 1], FILL_K0 + 2 * i, qk_made)
                if t == 23:
                    dve.wait_ge(chunk_used, at + 24)
                    dve.tensor_scalar(v[:, 1, :], acc[1][1][:], inv_rms[:, 0, 1:2], None, ALU.mult).then_inc(v_made, 1)

            def add_x(at, t, s, n):
                dve.wait_ge(chunk_used, at + t + 1)
                for b in range(BLK):
                    cols = slice(n * NC_, (n + 1) * NC_)
                    dve.tensor_tensor(xs[:, b, cols], acc[s][b][:], xs[:, b, cols], ALU.add).then_inc(x_added, 1)

            def gate_a(at, t, n):
                dve.wait_ge(chunk_used, at + t + 1)
                dve.wait_ge(sig_made, 4 * n + 2)
                dve.wait_ge(stage_turned, FILL_SLAB + n)
                for b in range(BLK):
                    dve.tensor_tensor(stage[:, b, :], acc[0][b][:], sig_a[:, b, :], ALU.mult).then_inc(gated_a, 1)

            def gate_b(at, t, n):
                dve.wait_ge(chunk_used, at + t + 1)
                dve.wait_ge(sig_made, 4 * n + 4)
                for b in range(BLK):
                    dve.tensor_tensor(sig_b[:, b, :], acc[1][b][:], sig_b[:, b, :], ALU.mult).then_inc(gated_b, 1)
                dve.wait_ge(gated_a, 2 * n + 2)
                dve.wait_ge(gated_b, 2 * n + 2)
                dve.tensor_tensor(stage[:], stage[:], sig_b, ALU.add).then_inc(merged, 1)

            norm_chain = Chain(norm_step)

            def mean_rows(which, b=None):
                rows = slice(0, BLK) if b is None else slice(b, b + 1)
                dve.wait_ge(squares, 2 * N_OUT * (which + 1) - (0 if b is None else 2 * (BLK - 1 - b)))
                norm_chain.then(dve.tensor_reduce(norm[:, which, 2, rows], sq[:, which, rows], AX.X, ALU.add))
                dve.tensor_scalar(norm[:, which, 0, rows], norm[:, which, 2, rows], 1.0 / D, EPS, ALU.mult, ALU.add) \
                    .then_inc(mean_made, 1)

            def inv_rows(which, b=None):
                rows = slice(0, BLK) if b is None else slice(b, b + 1)
                dve.wait_ge(root_made, which + 1 + (b or 0))
                w = norm[:, which, :, rows]
                norm_chain.then(dve.reciprocal(w[:, 3], w[:, 1]))
                norm_chain.then(dve.tensor_tensor(w[:, 4], w[:, 3], w[:, 3], ALU.mult))
                norm_chain.then(dve.tensor_tensor(w[:, 5], w[:, 4], w[:, 0], ALU.mult))
                norm_chain.then(dve.tensor_scalar(w[:, 2], w[:, 5], -0.5, 1.5, ALU.mult, ALU.add))
                dve.tensor_tensor(w[:, 6], w[:, 3], w[:, 2], ALU.mult).then_inc(scale_made, 1)
                dve.wait_ge(scale_made, which + 1 + (b or 0))

            def lo_rows(which, q, part=range(4)):
                for k in (4 * q + j for j in part):
                    dve.wait_ge(h_hi_made, KT * which + k // 2 * 2 + 2)
                    dve.scalar_tensor_tensor(out=h_lo[:, k, :], in0=four[k // 2 % 4][:, k % 2 * SEQ:(k % 2 + 1) * SEQ],
                                             scalar=g_cols[:, KT * which + k:KT * which + k + 1],
                                             in1=h_hi[:, k, :].bitcast(f32), op0=ALU.mult,
                                             op1=ALU.subtract).then_inc(h_made, 1)

            def bias_row(g):
                n = 4 if g < 3 else 8
                dve.wait_ge(bias_rows_made, g + 1)
                dve.tensor_copy(rows_sb[0:n, g, :], dots[g % 2][0:n, 0:SKEW]).then_inc(bias_rows_out, 1)

            dve.memset(warm[:, 0:1], 0.0).then_inc(warm_made, 1)
            dve.wait_ge(g_turned, 1)
            dve.tensor_copy(g_cols[:, 0:KT], acc[0][0][:, 0:KT]).then_inc(g_out, 1)
            dve.wait_ge(g_out, 1)
            lo_rows(0, 0, (0, 1))
            lo(IDX_AT, 0)
            lo_rows(0, 0, (2, 3))
            lo(IDX_AT, 1)
            lo(IDX_AT, 2)

            for t in range(IDX_LEN):
                lo(IDX_AT, t + AHEAD, width=KIW if 8 <= t + AHEAD < 16 else NC_)
                if t in (0, 2, 4):
                    lo_rows(0, 1 + t // 2)
                if t == 4:
                    dve.wait_ge(g_turned, 2)
                    dve.tensor_copy(g_cols[:, KT:2 * KT], acc[1][1][:, 0:KT]).then_inc(g_out, 1)
                    mean_rows(0)
                if t == 5:
                    inv_rows(0)
                if t == 7:
                    copy_stage(IDX_AT + 7, 0, FILL_QI[0])
                if t == 9:
                    copy_turned(qi_t[:, 0:4], FILL_QI[0], qi_t_made)
                if t in (10, 11, 18, 19):
                    bias_row((10, 11, 18, 19).index(t))
                if t == 15:
                    dve.wait_ge(chunk_used, IDX_AT + 16)
                    dve.tensor_copy(ki_cols, acc[1][0][0:KIW, 0:SEQ]).then_inc(ki_cols_made, 1)
                if t == 17:
                    dve.wait_ge(ki_rows_turned, 1)
                    for b in range(BLK):
                        inv = inv_rms[:, 0, b:b + 1]
                        for half in range(2):
                            dve.tensor_scalar(ki_twice[:, b, half * IDX:(half + 1) * IDX], tp[b][:, 0:IDX],
                                              inv, None, ALU.mult).then_inc(ki_made, 1)
                        dve.tensor_scalar(w_idx[:, b, :], tp[b][:, IDX:KIW], inv,
                                          (IDX ** -0.5) * (N_IDX ** -0.5), ALU.mult, ALU.mult).then_inc(w_idx_made, 1)
                if t == 19:
                    dve.wait_ge(ki_turned, 1)
                    dve.tensor_copy(ki_t[:, P:SEQ], tp[1][:, 0:P]).then_inc(ki_t_made, 1)
                if t == 23:
                    copy_stage(IDX_AT + 23, 0, FILL_QI[1])

            halves = ((0, slice(0, P)), (1, slice(P, SKEW)))

            def top_round(left, r):
                for b, cols in halves:
                    dve.max(top[:, b, :], left[:, cols]).then_inc(top_step, 1)
                dve.wait_ge(top_step, 4 * r + 2)
                for b, cols in halves:
                    dve.match_replace(out=idx_left[:, cols], in_to_replace=top[:, b, :], in_values=left[:, cols],
                                      imm_value=TAKEN).then_inc(top_step, 1)
                dve.wait_ge(top_step, 4 * r + 4)

            for t in range(QUAD_LEN):
                lo(QUAD_AT, t + AHEAD)
                if t == 1:
                    copy_turned(qi_t[:, 4:8], FILL_QI[1], qi_t_made)
                if 2 <= t < 2 + N_IDX:
                    h = t - 2
                    if h == 0:
                        dve.wait_ge(idx_zero, 3)
                    else:
                        dve.wait_ge(idx_added, 2 * h)
                    dve.wait_ge(relu_made, h + 1)
                    for b, cols in halves:
                        dve.scalar_tensor_tensor(out=idx_score[:, cols], in0=relu[h % 2][:, cols],
                                                 scalar=w_idx[:, b, h:h + 1], in1=idx_score[:, cols],
                                                 op0=ALU.mult, op1=ALU.add).then_inc(idx_added, 1)
                quad(QUAD_AT, 0, t)
                if t == 19:
                    dve.wait_ge(idx_added, 2 * N_IDX)
                if t in (19, 20, 21):
                    top_round(idx_left if t > 19 else idx_score, t - 19)

            def quad_pass(i, top_rounds=()):
                at = QUAD_AT + QUAD_LEN * i
                attend(i - 1, -1)
                for t in range(QUAD_LEN):
                    lo(at, t + AHEAD)
                    attend(i - 1, t)
                    quad(at, i, t)
                    if t in top_rounds:
                        top_round(idx_left, 3 + top_rounds.index(t))

            dve.wait_ge(bias_loaded, 2 * N_QUAD * 16)
            with dve.Fori(1, N_GROUP_A) as i:
                quad_pass(i)
            quad_pass(N_GROUP_A, (11, 12, 13, 14, 16))
            dve.wait_ge(bias_chosen, N_QUAD_B * QUAD)
            quad_pass(N_QUAD - 1)

            mix_chain = Chain(mix_step)

            def spread(weights):
                return weights.unsqueeze(2).to_broadcast([P, BLK * QUAD, HD])

            def heads(rows):
                return rows.rearrange("p b (j d) -> p (b j) d", j=QUAD)

            attend(N_QUAD - 1, -1)
            for t in range(MERGE3_LEN):
                nxt = t + AHEAD
                lo(MERGE0_AT, nxt, MERGE3_KTS[nxt] if nxt < MERGE3_LEN else 2)
                attend(N_QUAD - 1, t)
                if t == 6:
                    dve.wait_ge(u_made, 4 * N_GROUP_A)
                    mix_chain.then(dve.tensor_tensor(mix[:, 0, :], neg_max[:, 0, :], neg_max[:, 1, :], ALU.min))
                    mix_chain.then(dve.tensor_tensor(mix[:, 0, :], mix[:, 0, :], neg_max[:, 2, :], ALU.min))
                    for g in range(N_GROUP_A):
                        ins = dve.tensor_tensor(mix[:, 1 + g, :], mix[:, 0, :], neg_max[:, g, :], ALU.subtract)
                        if g < N_GROUP_A - 1:
                            mix_chain.then(ins)
                    ins.then_inc(mix_in, 1)
                if t == 8:
                    dve.wait_ge(mix_exp, 1)
                    mix_chain.then(dve.tensor_tensor(mix[:, 1:4, :], mix[:, 4:7, :], denom[:, 0:3, :], ALU.mult))
                    mix_chain.then(dve.tensor_tensor(mix[:, 0, :], mix[:, 1, :], mix[:, 2, :], ALU.add))
                    mix_chain.then(dve.tensor_tensor(mix[:, 0, :], mix[:, 0, :], mix[:, 3, :], ALU.add))
                    mix_chain.then(dve.reciprocal(mix[:, 7, :], mix[:, 0, :]))
                    for g in range(N_GROUP_A):
                        mix_chain.then(dve.tensor_tensor(mix[:, 4 + g, :], mix[:, 4 + g, :], mix[:, 7, :], ALU.mult))
                if t in (8, 9, 10):
                    g = t - 8
                    mix_chain.then(dve.tensor_tensor(heads(u[:, g]), heads(u[:, g]), spread(mix[:, 4 + g, :]),
                                                     ALU.mult))
                if t == 10:
                    mix_chain.then(dve.tensor_tensor(u[:, 0], u[:, 0], u[:, 1], ALU.add))
                if t == 11:
                    dve.wait_ge(stage_turned, FILL_Y)
                    dve.tensor_tensor(stage[:], u[:, 0], u[:, 2], ALU.add).then_inc(stage_made, 2)
                    dve.wait_ge(u_made, N_HEADS)
                    mix_chain.then(dve.reciprocal(mix[:, 0:2, :], denom[:, 3:5, :]))
                if t == 13:
                    lo_turned(y_lo[:, 0:QUAD], y_hi[:, 0:QUAD], FILL_Y, y_made)
                if t in (13, 15):
                    n = (t - 13) // 2
                    dve.wait_ge(stage_turned, FILL_Y + 1 + n)
                    dve.tensor_tensor(heads(stage[:]), heads(u[:, 3 + n]), spread(mix[:, n, :]), ALU.mult) \
                        .then_inc(stage_made, 2)
                if t in (15, 17):
                    n = (t - 13) // 2
                    lo_turned(y_lo[:, QUAD * n:QUAD * (n + 1)], y_hi[:, QUAD * n:QUAD * (n + 1)], FILL_Y + n, y_made)
                if t == 18:
                    gate_a(MERGE0_AT, t, 0)
                if t == 23:
                    gate_b(MERGE0_AT, t, 0)
            with dve.Fori(1, N_OUT - 1) as n:
                at = (MERGE_AT - MERGE_LEN) + MERGE_LEN * n
                for t in range(MERGE_LEN):
                    nxt = t + AHEAD
                    lo(at, nxt, MERGE_KTS[nxt] if nxt < MERGE_LEN else 2)
                    if t == 2:
                        lo_turned(slab_lo[:], slab_hi, FILL_SLAB - 1 + n, slab_made)
                    if t in (9, 11, 13, 15):
                        add_x(at, t, (t - 7) // 2 % 2, (t - 9) // 2)
                    if t == 26:
                        gate_a(at, t, n)
                    if t == 31:
                        gate_b(at, t, n)
            for t in range(MERGE3_LEN):
                nxt = t + AHEAD
                lo(MERGE3_AT, nxt, MERGE3_KTS[nxt] if nxt < MERGE3_LEN else 2)
                if t == 2:
                    lo_turned(slab_lo[:], slab_hi, FILL_SLAB + N_OUT - 2, slab_made)
                if t == 18:
                    gate_a(MERGE3_AT, t, N_OUT - 1)
                if t == 23:
                    gate_b(MERGE3_AT, t, N_OUT - 1)
            for t in range(WOUT_LEN):
                lo(WOUT_AT, t + AHEAD)
                if t == 2:
                    lo_turned(y_lo[:, 0:QUAD], y_hi[:, 0:QUAD], FILL_SLAB + N_OUT - 1, slab_made)
                if t % 2:
                    add_x(WOUT_AT, t, t // 2 % 2, t % 8 // 2)
                if t in (11, 13, 15):
                    lo_rows(1, (t - 11) // 2)

            def swiglu(at, t, i):
                dve.wait_ge(chunk_used, at + t + 1)
                dve.wait_ge(silu_made, 2 * i + 2)
                dve.wait_ge(stage_turned, FILL_SLAB + N_OUT + i)
                for b in range(BLK):
                    dve.scalar_tensor_tensor(out=stage[:, b, :], in0=acc[1][b][:], scalar=inv_rms[:, 1, b:b + 1],
                                             in1=silu[:, b, :], op0=ALU.mult, op1=ALU.mult).then_inc(swiglu_made, 1)

            for t in range(FFN0_LEN):
                lo(FFN0_AT, t + AHEAD)
                if t == 1:
                    lo_rows(1, 3)
                    mean_rows(1)
                if t == 3:
                    inv_rows(1)
                if t == 15:
                    swiglu(FFN0_AT, t, 0)
            with dve.Fori(1, N_SLAB - 1) as i:
                at = (FFN_AT - FFN_LEN) + FFN_LEN * i
                for t in range(FFN_LEN):
                    lo(at, t + AHEAD)
                    if t == 2:
                        lo_turned(slab_lo[:], slab_hi, FILL_SLAB + N_OUT - 1 + i, slab_made)
                    if t in (9, 11, 13, 15):
                        add_x(at, t, (t - 7) // 2 % 2, (t - 9) // 2)
                    if t == 23:
                        swiglu(at, t, i)
            for t in range(FFN0_LEN):
                lo(FFN10_AT, t + AHEAD)
                if t == 2:
                    lo_turned(slab_lo[:], slab_hi, FILL_SLAB + N_OUT + N_SLAB - 2, slab_made)
                if t == 15:
                    swiglu(FFN10_AT, t, N_SLAB - 1)
            def weigh(b, n):
                cols = slice(n * NC_, (n + 1) * NC_)
                dve.tensor_tensor(xg[:, b, cols], xs[:, b, cols], g_last[:, cols], ALU.mult).then_inc(xg_made, 1)

            dve.wait_ge(g_last_loaded, 16)
            for t in range(DOWN_LEN):
                if t + AHEAD < DOWN_LEN:
                    lo(DOWN_AT, t + AHEAD)
                if t == 2:
                    lo_turned(y_lo[:, 0:QUAD], y_hi[:, 0:QUAD], FILL_SLAB + N_OUT + N_SLAB - 1, slab_made)
                if t % 2 and t < DOWN_LEN - RING:
                    add_x(DOWN_AT, t, t // 2 % 2, t % 8 // 2)
                if t in (10, 12):
                    dve.wait_ge(x_added, 2 * N_OUT * (N_OUT + N_SLAB - 1) + t - 8)
                    for b in range(BLK):
                        weigh(b, (t - 10) // 2)
            for b in range(BLK):
                for s in range(2):
                    n = N_OUT - 2 + s
                    cols = slice(n * NC_, (n + 1) * NC_)
                    dve.wait_ge(last_made, 2 * b + s + 1)
                    dve.tensor_tensor(xs[:, b, cols], acc[s][b][:], xs[:, b, cols], ALU.add).then_inc(x_added, 1)
                    dve.wait_ge(x_added, 2 * N_OUT * (N_OUT + N_SLAB) - 2 * BLK + 2 * b + s + 1)
                    weigh(b, n)
                mean_rows(2, b)
                inv_rows(2, b)
                dve.wait_ge(xg_made, 2 * (N_OUT - 2) + 2 * (b + 1))
                dve.tensor_scalar(xg[:, b, 0:D // 2], xg[:, b, 0:D // 2], inv_rms[:, 2, b:b + 1], None, ALU.mult) \
                    .then_inc(out_left_made, 1)

        @block.tensor
        def _(pe):
            def chunk(at, t, x_hi, x_lo, k0, s, first, last, kts=2, width=NC_):
                slot = t % RING
                pe.wait_ge(lo_made, at + t + 1)
                for k in range(kts):
                    for b in range(BLK):
                        rows = slice(b * P, (b + 1) * P)
                        dst = acc[s][b][:, 0:width]
                        a_hi, a_lo = x_hi[:, k0 + k, rows], x_lo[:, k0 + k, rows]
                        b_hi, b_lo = w_hi[:, slot, k, 0:width], w_lo[:, slot, k, 0:width]
                        pe.matmul(dst, a_hi, b_hi, start=first and k == 0, stop=False)
                        pe.matmul(dst, a_hi, b_lo, start=False, stop=False)
                        ins = pe.matmul(dst, a_lo, b_hi, start=False, stop=last and k == kts - 1)
                ins.then_inc(chunk_used, 1)

            def column_chunk(at, t, j, s, free, width=NC_, h_from=None):
                if j == 0:
                    for f in free:
                        pe.wait_ge(*f)
                if h_from is not None:
                    pe.wait_ge(h_made, h_from + 2 * j + 2)
                chunk(at, t, h_hi, h_lo, 2 * j, s, j == 0, j == KT // 2 - 1, width=width)

            def slab_chunk(at, t, j, s, free, hi=slab_hi, lo=slab_lo):
                if j % 2 == 0:
                    for f in free:
                        pe.wait_ge(*f)
                chunk(at, t, hi, lo, j % 2 * 2, s, j % 2 == 0, j % 2 == 1)

            def turn(made, free):
                pe.wait_ge(*made)
                for f in free:
                    pe.wait_ge(*f)
                for b in range(BLK):
                    for j in range(QUAD):
                        ins = pe.transpose(tp[b][:, j * P:(j + 1) * P], stage[:, b, j * P:(j + 1) * P], ident[:])
                ins.then_inc(stage_turned, 1)

            def qk_product(a, j):
                if j < 2:
                    pe.wait_ge(qk_made, 4 * a + 4)
                else:
                    pe.wait_ge(biased, 4 * a + j - 1)
                dst = tp[j % 2]
                pe.matmul(dst[:, 0:P], qk[:, 0, j, 0:P], qk[:, 1, j, 0:P], start=True, stop=True)
                pe.matmul(dst[:, P:SKEW], qk[:, 0, j, P:SEQ], qk[:, 1, j, :], start=True, stop=True) \
                    .then_inc(scored, 1)

            def prob_turn(a, j):
                pe.wait_ge(exp_made, 8 * a + 2 * j + 2)
                if j:
                    pe.wait_ge(prob_t_made, 4 * a + j)
                for n in range(3):
                    cols = slice(n * P, (n + 1) * P)
                    ins = pe.transpose(pt[:, cols], prob[j % 2][:, cols], ident[:])
                ins.then_inc(prob_turned, 1)

            def pv_product(a, j):
                pe.wait_ge(prob_t_made, 4 * a + j + 1)
                pe.wait_ge(v_made, 2 * a + 2)
                if j:
                    pe.wait_ge(u_made, 4 * a + j)
                cols = slice(j * HD, (j + 1) * HD)
                pe.matmul(po[:, 0:P], prob_t[j % 2][:, 0:P], v[:, 0, cols], start=True, stop=True)
                pe.matmul(po[:, P:SEQ], prob_t[j % 2][:, P:2 * P], v[:, 0, cols], start=True, stop=False)
                pe.matmul(po[:, P:SEQ], prob_t[j % 2][:, 2 * P:SKEW], v[:, 1, cols], start=False, stop=True) \
                    .then_inc(pv_made, 1)

            def attend(a, t):
                if t == -1:
                    qk_product(a, 0)
                    qk_product(a, 1)
                if t in (3, 5, 7, 9):
                    pv_product(a, (t - 3) // 2)
                if t in (1, 3, 5, 7):
                    prob_turn(a, (t - 1) // 2)
                if t in (2, 4):
                    qk_product(a, 2 + (t - 2) // 2)

            def quad_chunk(at, i, t, q_free, q_tp_free):
                if t < 8:
                    column_chunk(at, t, t, 1, q_free)
                elif t < 16:
                    column_chunk(at, t, t - 8, 0, [(stage_made, 4 * i + 4)])
                else:
                    column_chunk(at, t, t - 16, 1, [(stage_made, 4 * i + 6)])
                if t == 10:
                    turn((stage_made, 2 * (FILL_Q0 + 2 * i) + 2), q_tp_free)
                if t == 18:
                    turn((stage_made, 2 * (FILL_K0 + 2 * i) + 2), [(qk_made, 4 * i + 2)])

            def turn_rows(which, q, free):
                for f in free:
                    pe.wait_ge(*f)
                if q >= 2:
                    pe.wait_ge(h_made, KT * which + 4 * (q - 1))
                for k in range(4 * q, 4 * q + 4):
                    for b in range(BLK):
                        ins = pe.transpose(four[k // 2 % 4][:, k % 2 * SEQ + b * P:k % 2 * SEQ + (b + 1) * P],
                                           xs[:, b, k * P:(k + 1) * P], ident[:])
                    ins.then_inc(h_turned, 1)

            pe.wait_ge(g_mix_loaded, 16)
            pe.wait_ge(ident_made, 1)
            pe.transpose(acc[0][0][:, 0:KT], g_rows[0][:], ident[0:KT, 0:KT]).then_inc(g_turned, 1)
            turn_rows(0, 0, [(x_loaded[0], 16)])

            for t in range(IDX_LEN):
                if t < 8:
                    column_chunk(IDX_AT, t, t, 0, [(g_out, 1)], h_from=0)
                elif t < 16:
                    slot = t % RING
                    pe.wait_ge(lo_made, IDX_AT + t + 1)
                    for k in range(2):
                        dst, j = acc[1][0][0:KIW, 0:SEQ], 2 * (t - 8) + k
                        b_hi, b_lo = w_hi[:, slot, k, 0:KIW], w_lo[:, slot, k, 0:KIW]
                        pe.matmul(dst, b_hi, h_hi[:, j, :], start=j == 0, stop=False)
                        pe.matmul(dst, b_hi, h_lo[:, j, :], start=False, stop=False)
                        ins = pe.matmul(dst, b_lo, h_hi[:, j, :], start=False, stop=j == KT - 1)
                    ins.then_inc(chunk_used, 1)
                else:
                    column_chunk(IDX_AT, t, t - 16, 0, [(stage_made, 2)])
                if t in (0, 2, 4):
                    turn_rows(0, 1 + t // 2, [(x_loaded[1 + t // 2], 16)])
                if t == 0:
                    pe.wait_ge(g_ffn_loaded, 16)
                    pe.transpose(acc[1][1][:, 0:KT], g_rows[1][:], ident[0:KT, 0:KT]).then_inc(g_turned, 1)
                if t == 9:
                    turn((stage_made, 2), [(h_made, KT)])
                if t in (10, 11, 18, 19):
                    g = (10, 11, 18, 19).index(t)
                    n = 4 if g < 3 else 8
                    if g == 0:
                        pe.wait_ge(hot_loaded, 16)
                        pe.wait_ge(rel_loaded, 16)
                        pe.wait_ge(rel_masked, 1)
                    if g >= 2:
                        pe.wait_ge(bias_rows_out, g - 1)
                    pe.matmul(dots[g % 2][0:n, 0:SKEW], rel[:, 4 * g:4 * g + n], hot[:, g, :],
                              start=True, stop=True).then_inc(bias_rows_made, 1)
                if t == 17:
                    pe.wait_ge(ki_cols_made, 1)
                    pe.wait_ge(qi_t_made, 2)
                    for b in range(BLK):
                        ins = pe.transpose(tp[b][:, 0:KIW], ki_cols[:, b * P:(b + 1) * P], ident[0:KIW, 0:KIW])
                    ins.then_inc(ki_rows_turned, 1)
                if t == 19:
                    pe.wait_ge(ki_made, 4)
                    pe.wait_ge(w_idx_made, 2)
                    for b in range(BLK):
                        ins = pe.transpose(tp[b][:, 0:P], ki_twice[:, b, :], ident[:])
                    ins.then_inc(ki_turned, 1)

            for t in range(QUAD_LEN):
                quad_chunk(QUAD_AT, 0, t, [(ki_cols_made, 1)], [(qi_t_made, 4)])
                if t == 1:
                    turn((stage_made, 4), [(ki_t_made, 2)])
                if 2 <= t < 2 + N_IDX:
                    h = t - 2
                    pe.wait_ge(qi_t_made, 2 if h < 8 else 4)
                    if h == 0:
                        pe.wait_ge(bias_rows_out, 4)
                    if h >= 2:
                        pe.wait_ge(relu_made, h - 1)
                    half = slice(h % 2 * IDX, (h % 2 + 1) * IDX)
                    pe.matmul(dots[h % 2][:, 0:P], qi_t[half, h // 2, 0:P], ki_t[half, 0:P], start=True, stop=True)
                    pe.matmul(dots[h % 2][:, P:SKEW], qi_t[half, h // 2, P:SEQ], ki_t[half, :],
                              start=True, stop=True).then_inc(dots_made, 1)

            pe.wait_ge(relu_made, N_IDX)
            with pe.Fori(1, N_QUAD) as i:
                at = QUAD_AT + QUAD_LEN * i
                attend(i - 1, -1)
                for t in range(QUAD_LEN):
                    quad_chunk(at, i, t, [(v_made, 2 * i)], [(biased, 4 * i)])
                    attend(i - 1, t)

            def y_chunk(at, t, t0, s, kts, k0, free):
                j = t - t0
                if j == 0:
                    for f in free:
                        pe.wait_ge(*f)
                chunk(at, t, y_hi, y_lo, k0 + sum(kts[:j]), s, j == 0, j == len(kts) - 1, kts[j])

            attend(N_QUAD - 1, -1)
            for t in range(MERGE3_LEN):
                if t < 8:
                    column_chunk(MERGE0_AT, t, t, 0, [(stage_made, 2 * (FILL_K0 + 2 * N_QUAD - 1))])
                elif t < 16:
                    column_chunk(MERGE0_AT, t, t - 8, 1, [(v_made, 2 * N_QUAD)])
                elif t < 19:
                    y_chunk(MERGE0_AT, t, 16, 0, YA_KTS, 0, [(sig_made, 2), (y_made, 2)])
                else:
                    y_chunk(MERGE0_AT, t, 19, 1, YB_KTS, QUAD, [(sig_made, 4), (y_made, 6)])
                attend(N_QUAD - 1, t)
                if t == 13:
                    turn((stage_made, 2 * FILL_Y + 2), [(biased, N_HEADS)])
                if t in (15, 17):
                    n = (t - 13) // 2
                    turn((stage_made, 2 * (FILL_Y + n) + 2), [(y_made, 2 * n)])
            with pe.Fori(1, N_OUT - 1) as n:
                at = (MERGE_AT - MERGE_LEN) + MERGE_LEN * n
                added = 2 * N_OUT * n - 2 * N_OUT
                w_free = ((gated_b, 2 * n), (sig_made, 4 * n + 2), (x_added, added + 2), (x_added, added + 4))
                for t in range(MERGE_LEN):
                    if t < 8:
                        column_chunk(at, t, t, 0, [(gated_a, 2 * n)])
                    elif t < 16:
                        if t == 8:
                            pe.wait_ge(slab_made, 2 * n)
                        slab_chunk(at, t, t - 8, (t - 6) // 2 % 2, [w_free[(t - 8) // 2]])
                    elif t < 24:
                        column_chunk(at, t, t - 16, 1, [(x_added, added + 6)])
                    elif t < 27:
                        y_chunk(at, t, 24, 0, YA_KTS, 0, [(x_added, added + 8)])
                    else:
                        y_chunk(at, t, 27, 1, YB_KTS, QUAD, [(sig_made, 4 * n + 4)])
                    if t == 2:
                        turn((merged, n), [(y_made, 6)])
            n = N_OUT - 1
            for t in range(MERGE3_LEN):
                if t < 8:
                    column_chunk(MERGE3_AT, t, t, 0, [(gated_a, 2 * n)])
                elif t < 16:
                    column_chunk(MERGE3_AT, t, t - 8, 1, [(gated_b, 2 * n)])
                elif t < 19:
                    y_chunk(MERGE3_AT, t, 16, 0, YA_KTS, 0, [(sig_made, 4 * n + 2)])
                else:
                    y_chunk(MERGE3_AT, t, 19, 1, YB_KTS, QUAD, [(sig_made, 4 * n + 4)])
                if t == 2:
                    turn((merged, n), [(slab_made, 2 * (n - 1))])

            def last_slabs(at, t, before, before2, made):
                w_free = (*before2, *((x_added, before + n) for n in range(2, 14, 2)))[t // 2]
                if t % 8 == 0:
                    pe.wait_ge(slab_made, made + 2 * (t // 8))
                x_hi, x_lo = ((slab_hi, slab_lo), (y_hi, y_lo))[t // 8]
                slab_chunk(at, t, t % 8, t // 2 % 2, [w_free], x_hi, x_lo)

            for t in range(WOUT_LEN):
                last_slabs(WOUT_AT, t, 2 * N_OUT * (N_OUT - 2), ((gated_a, 2 * N_OUT), (gated_b, 2 * N_OUT)),
                           2 * (N_OUT - 1))
                if t == 2:
                    turn((merged, N_OUT), [(slab_made, 2 * (N_OUT - 1))])
                if t in (11, 13, 15):
                    q = (t - 11) // 2
                    turn_rows(1, q, [(x_added, 2 * N_OUT * (N_OUT - 1) + 2 * q + 2),
                                     *([(slab_made, 2 * N_OUT)], [(prob_t_made, N_HEADS), (u_made, N_HEADS)], [])[q]])

            added0 = 2 * N_OUT * N_OUT
            for t in range(FFN0_LEN):
                column_chunk(FFN0_AT, t, t % 8, t // 8, [(x_added, added0 - 2 + 2 * (t // 8))],
                             h_from=KT if t < 8 else None)
                if t == 1:
                    turn_rows(1, 3, [(x_added, added0)])
            with pe.Fori(1, N_SLAB - 1) as i:
                at = (FFN_AT - FFN_LEN) + FFN_LEN * i
                added = (added0 - 2 * N_OUT) + 2 * N_OUT * i
                w_free = ((swiglu_made, 2 * i), (silu_made, 2 * i + 2), (x_added, added + 2), (x_added, added + 4))
                for t in range(FFN_LEN):
                    if t < 8:
                        column_chunk(at, t, t, 0, [(x_added, added), (silu_made, 2 * i)])
                    elif t < 16:
                        if t == 8:
                            pe.wait_ge(slab_made, 2 * N_OUT + 2 * i)
                        slab_chunk(at, t, t - 8, (t - 6) // 2 % 2, [w_free[(t - 8) // 2]])
                    else:
                        column_chunk(at, t, t - 16, 1, [(x_added, added + 6)])
                    if t == 2:
                        turn((swiglu_made, 2 * i), [(slab_made, 2 * (N_OUT - 1) + 2 * i), (h_made, 2 * KT)])
            i = N_SLAB - 1
            before = added0 + 2 * N_OUT * (N_SLAB - 2)
            for t in range(FFN0_LEN):
                column_chunk(FFN10_AT, t, t % 8, t // 8, [(x_added, before) if t < 8 else (swiglu_made, 2 * i)])
                if t == 2:
                    turn((swiglu_made, 2 * i), [(slab_made, 2 * (N_OUT - 1) + 2 * i)])
            for t in range(DOWN_LEN - RING):
                last_slabs(DOWN_AT, t, before, ((silu_made, 2 * N_SLAB), (swiglu_made, 2 * N_SLAB)),
                           2 * (N_OUT + N_SLAB - 1))
                if t == 2:
                    turn((swiglu_made, 2 * N_SLAB), [(slab_made, 2 * (N_OUT + N_SLAB - 1))])
            for b in range(BLK):
                for s in range(2):
                    if b == 0:
                        pe.wait_ge(x_added, before + 2 * N_OUT + 2 * s + 2)
                    for j in range(4):
                        c = DOWN_LEN - RING + 2 * s + j // 2
                        if b == 0 and j % 2 == 0:
                            pe.wait_ge(lo_made, DOWN_AT + c + 1)
                        x_hi, x_lo = y_hi[:, j, b * P:(b + 1) * P], y_lo[:, j, b * P:(b + 1) * P]
                        b_hi, b_lo = w_hi[:, c % RING, j % 2, :], w_lo[:, c % RING, j % 2, :]
                        pe.matmul(acc[s][b][:], x_hi, b_hi, start=j == 0, stop=False)
                        pe.matmul(acc[s][b][:], x_hi, b_lo, start=False, stop=False)
                        ins = pe.matmul(acc[s][b][:], x_lo, b_hi, start=False, stop=j == 3)
                    ins.then_inc(last_made, 1)


def bucket_rows():
    dist = SEQ - 1 - np.arange(SKEW)
    far = np.maximum(dist, 1).astype(np.float32) / np.float32(BUCKETS // 2)
    large = BUCKETS // 2 + (np.log(far) / np.float32(np.log(2048 / (BUCKETS // 2)))
                            * np.float32(BUCKETS // 2)).astype(np.int32)
    bucket = np.where(dist < BUCKETS // 2, np.maximum(dist, 0), np.minimum(large, BUCKETS - 1))
    rows = np.zeros((BUCKETS + 1, 4, SKEW), np.float32)
    for g, (window, dilation) in enumerate(((128, 1), (512, 4), (2048, 16), (SEQ, 1))):
        seen = (dist >= 0) & (dist <= window) & (dist % dilation == 0)
        rows[np.where(seen, bucket, BUCKETS), g, np.arange(SKEW)] = 1.0
    return rows


_INS = ("x", "w_in", "w_out_a", "w_out_b", "w_out", "w_ff_gate", "w_ff_up", "w_ff_down", "g_mix", "g_ffn",
        "g_final", "rel_bias")


def kernel(**inputs):
    import concourse.bacc as bacc
    from concourse.bass_utils import run_bass_kernel_spmd

    nc = bacc.Bacc("TRN2", target_bir_lowering=False, num_devices=1)
    f32 = mybir.dt.float32
    arrays = {f"in_{name}": np.ascontiguousarray(inputs[name]) for name in _INS}
    arrays["in_onehot"] = bucket_rows()
    args = [nc.dram_tensor(name, a.shape, f32, kind="ExternalInput").ap() for name, a in arrays.items()]
    out = nc.dram_tensor("out", (1, SEQ, D), f32, kind="ExternalOutput").ap()
    bias_rows = nc.dram_tensor("bias_rows", (N_HEADS, P * (SKEW + 1)), f32, kind="Internal").ap()
    build(nc, *args, out, bias_rows)
    r = run_bass_kernel_spmd(nc, [arrays], core_ids=[0])
    return r.results[0]["out"]
```
